# Optimizing a Trainium2 kernel written in Bass

```python
import math
import jax, jax.numpy as jnp
from jax import lax
import numpy as np

D_MODEL = 2048
BATCH = 1
SEQ = 256
DEPTH = 1

N_Q_HEADS = 16
N_KV_HEADS = 4
Q_GROUP = N_Q_HEADS // N_KV_HEADS
HEAD_DIM = 128
WINDOW = 128
BLOCK = 128
ATTN_WIDTH = N_Q_HEADS * HEAD_DIM
KV_WIDTH = N_KV_HEADS * HEAD_DIM

SSM_WIDTH = D_MODEL // 2
SSM_GROUP = 16
SSM_GROUPS = SSM_WIDTH // SSM_GROUP
SSM_STATE = 64
DT_MIN = 1e-3
DT_MAX = 1e-1

PEER_HEADS = 8
N_KEYS = 128
N_EXPERTS = N_KEYS * N_KEYS
PEER_QDIM = 256
PEER_HALF = PEER_QDIM // 2
PEER_TOPK = 16
PEER_TOKEN_BLOCK = 128

RMS_EPS = 1e-6
IN_WIDTH = ATTN_WIDTH + 2 * KV_WIDTH + SSM_WIDTH + 2 * D_MODEL
IN_SPLITS = (ATTN_WIDTH, ATTN_WIDTH + KV_WIDTH, ATTN_WIDTH + 2 * KV_WIDTH,
             ATTN_WIDTH + 2 * KV_WIDTH + SSM_WIDTH,
             ATTN_WIDTH + 2 * KV_WIDTH + SSM_WIDTH + D_MODEL)


def rms_norm(x, g):
    xf = x.astype(jnp.float32)
    y = xf * lax.rsqrt(jnp.mean(xf * xf, axis=-1, keepdims=True) + RMS_EPS)
    return (y * g.astype(jnp.float32)).astype(x.dtype)

def alibi_slopes(n_heads):
    return jnp.exp2(-8.0 * (jnp.arange(n_heads, dtype=jnp.float32) + 1.0) / n_heads)

def windowed_gqa(q, k, v, sink):
    b_, s_ = q.shape[0], q.shape[1]
    nb = s_ // BLOCK
    qb = q.reshape(b_, nb, BLOCK, N_KV_HEADS, Q_GROUP, HEAD_DIM).transpose(1, 0, 2, 3, 4, 5)
    pad = ((0, 0), (BLOCK, BLOCK), (0, 0), (0, 0))

    def band(t):
        tp = jnp.pad(t, pad).reshape(b_, nb + 2, BLOCK, N_KV_HEADS, HEAD_DIM)
        tw = jnp.concatenate([tp[:, :-2], tp[:, 1:-1], tp[:, 2:]], axis=2)
        return tw.transpose(1, 0, 2, 3, 4)

    kw, vw = band(k), band(v)
    slopes = alibi_slopes(N_Q_HEADS).reshape(N_KV_HEADS, Q_GROUP)[:, :, None, None]
    sink_f = sink.astype(jnp.float32).reshape(N_KV_HEADS, Q_GROUP)[:, :, None, None]
    scale = HEAD_DIM ** -0.5

    def block_attn(args):
        blk, qi, ki, vi = args
        qpos = blk * BLOCK + jnp.arange(BLOCK)
        kpos = (blk - 1) * BLOCK + jnp.arange(3 * BLOCK)
        dist = jnp.abs(qpos[:, None] - kpos[None, :])
        valid = (dist <= WINDOW) & (kpos >= 0) & (kpos < s_)
        s = jnp.einsum('bqkgd,bskd->bkgqs', qi.astype(jnp.float32), ki.astype(jnp.float32)) * scale
        s = s - slopes * dist.astype(jnp.float32)
        s = jnp.where(valid, s, -jnp.inf)
        m = jnp.maximum(jnp.max(s, axis=-1, keepdims=True), sink_f)
        p = jnp.exp(s - m)
        denom = jnp.sum(p, axis=-1, keepdims=True) + jnp.exp(sink_f - m)
        o = jnp.einsum('bkgqs,bskd->bqkgd', p / denom, vi.astype(jnp.float32))
        return o.astype(q.dtype)

    out = lax.map(block_attn, (jnp.arange(nb), qb, kw, vw))
    return out.transpose(1, 0, 2, 3, 4, 5).reshape(b_, s_, ATTN_WIDTH)

def _ssm_combine(left, right):
    a_l, b_l = left
    a_r, b_r = right
    return a_r * a_l, a_r * b_l + b_r

def s5_direction(u, a_re, a_im, log_step, b_re, b_im, c_re, c_im, reverse):
    s_ = u.shape[1]
    lam = lax.complex(a_re.astype(jnp.float32), a_im.astype(jnp.float32))
    step = jnp.exp(log_step.astype(jnp.float32))[:, None]
    lam_bar = jnp.exp(lam * step)
    b_mat = lax.complex(b_re.astype(jnp.float32), b_im.astype(jnp.float32))
    b_bar = ((lam_bar - 1.0) / lam)[:, :, None] * b_mat
    bu = jnp.einsum('bsgc,gnc->bsgn', u.astype(jnp.complex64), b_bar)
    a = jnp.broadcast_to(lam_bar[None, None], (1, s_, SSM_GROUPS, SSM_STATE))
    _, states = lax.associative_scan(_ssm_combine, (a, bu), reverse=reverse, axis=1)
    c_mat = lax.complex(c_re.astype(jnp.float32), c_im.astype(jnp.float32))
    return jnp.real(jnp.einsum('bsgn,gcn->bsgc', states, c_mat))

def peer(h, w_query, sub_keys_1, sub_keys_2, expert_down, expert_up):
    b_, s_, d_ = h.shape
    t_ = b_ * s_
    ht = h.reshape(t_, d_)
    q = (ht @ w_query).astype(jnp.float32).reshape(t_, PEER_HEADS, 2, PEER_HALF)
    s1 = jnp.einsum('thd,hkd->thk', q[:, :, 0], sub_keys_1.astype(jnp.float32))
    s2 = jnp.einsum('thd,hkd->thk', q[:, :, 1], sub_keys_2.astype(jnp.float32))
    v1, i1 = lax.top_k(s1, PEER_TOPK)
    v2, i2 = lax.top_k(s2, PEER_TOPK)
    cand = (v1[..., :, None] + v2[..., None, :]).reshape(t_, PEER_HEADS, PEER_TOPK * PEER_TOPK)
    cand_idx = (i1[..., :, None] * N_KEYS + i2[..., None, :]).reshape(t_, PEER_HEADS, PEER_TOPK * PEER_TOPK)
    top_s, pos = lax.top_k(cand, PEER_TOPK)
    idx = jnp.take_along_axis(cand_idx, pos, axis=-1)
    gate = jax.nn.softmax(top_s, axis=-1)
    nblk = t_ // PEER_TOKEN_BLOCK
    k_sel = PEER_HEADS * PEER_TOPK
    xs = (ht.reshape(nblk, PEER_TOKEN_BLOCK, d_),
          idx.reshape(nblk, PEER_TOKEN_BLOCK, k_sel),
          gate.reshape(nblk, PEER_TOKEN_BLOCK, k_sel))

    def token_block(args):
        hb, ib, gb = args
        u_sel = jnp.take(expert_down, ib, axis=0)
        act = jnp.einsum('tkd,td->tk', u_sel.astype(jnp.float32), hb.astype(jnp.float32))
        w = gb * jax.nn.gelu(act, approximate=False)
        v_sel = jnp.take(expert_up, ib, axis=0)
        return jnp.einsum('tk,tkd->td', w, v_sel.astype(jnp.float32))

    return lax.map(token_block, xs).reshape(b_, s_, d_)

def first_inputs(seed: int = 0) -> dict:
    key = jax.random.key(seed)
    ks = jax.random.split(key, 24)
    L, D, f32 = DEPTH, D_MODEL, jnp.float32
    G, N, C = SSM_GROUPS, SSM_STATE, SSM_GROUP
    nrm = lambda k, shape, sc: jax.random.normal(k, shape, f32) * sc
    a_im_base = jnp.pi * jnp.arange(N, dtype=f32)
    return {
        "x": nrm(ks[0], (BATCH, SEQ, D), 1.0),
        "mix_norm_g": 1.0 + nrm(ks[1], (L, D), 0.02),
        "w_in": nrm(ks[2], (L, D, IN_WIDTH), D ** -0.5),
        "q_norm_g": 1.0 + nrm(ks[3], (L, HEAD_DIM), 0.02),
        "k_norm_g": 1.0 + nrm(ks[4], (L, HEAD_DIM), 0.02),
        "attn_sink": nrm(ks[5], (L, N_Q_HEADS), 0.5),
        "w_attn_o": nrm(ks[6], (L, ATTN_WIDTH, D), ATTN_WIDTH ** -0.5),
        "ssm_a_re": -0.5 + nrm(ks[7], (L, 2, G, N), 0.01),
        "ssm_a_im": a_im_base + nrm(ks[8], (L, 2, G, N), 0.01),
        "ssm_log_step": jax.random.uniform(ks[9], (L, 2, G), f32, math.log(DT_MIN), math.log(DT_MAX)),
        "ssm_b_re": nrm(ks[10], (L, 2, G, N, C), (2.0 * C) ** -0.5),
        "ssm_b_im": nrm(ks[11], (L, 2, G, N, C), (2.0 * C) ** -0.5),
        "ssm_c_re": nrm(ks[12], (L, 2, G, C, N), (2.0 * N) ** -0.5),
        "ssm_c_im": nrm(ks[13], (L, 2, G, C, N), (2.0 * N) ** -0.5),
        "ssm_d": nrm(ks[14], (L, SSM_WIDTH), 1.0),
        "glu_w_a": nrm(ks[15], (L, SSM_WIDTH, D), SSM_WIDTH ** -0.5),
        "glu_w_b": nrm(ks[16], (L, SSM_WIDTH, D), SSM_WIDTH ** -0.5),
        "w_out": nrm(ks[17], (L, D, D), D ** -0.5),
        "ffn_norm_g": 1.0 + nrm(ks[18], (L, D), 0.02),
        "peer_w_query": nrm(ks[19], (L, D, PEER_HEADS * PEER_QDIM), D ** -0.5),
        "peer_sub_keys_1": nrm(ks[20], (L, PEER_HEADS, N_KEYS, PEER_HALF), PEER_HALF ** -0.5),
        "peer_sub_keys_2": nrm(ks[21], (L, PEER_HEADS, N_KEYS, PEER_HALF), PEER_HALF ** -0.5),
        "peer_down": nrm(ks[22], (L, N_EXPERTS, D), D ** -0.5),
        "peer_up": nrm(ks[23], (L, N_EXPERTS, D), 0.25),
    }

def first_block(x, mix_norm_g, w_in, q_norm_g, k_norm_g, attn_sink, w_attn_o,
              ssm_a_re, ssm_a_im, ssm_log_step, ssm_b_re, ssm_b_im, ssm_c_re, ssm_c_im, ssm_d,
              glu_w_a, glu_w_b, w_out, ffn_norm_g, peer_w_query, peer_sub_keys_1,
              peer_sub_keys_2, peer_down, peer_up):
    b_, s_ = x.shape[0], x.shape[1]
    for l in range(DEPTH):
        h = rms_norm(x, mix_norm_g[l])
        proj = h @ w_in[l]
        q, k, v, u, gate_a, gate_b = jnp.split(proj, IN_SPLITS, axis=-1)
        q = rms_norm(q.reshape(b_, s_, N_Q_HEADS, HEAD_DIM), q_norm_g[l])
        k = rms_norm(k.reshape(b_, s_, N_KV_HEADS, HEAD_DIM), k_norm_g[l])
        v = v.reshape(b_, s_, N_KV_HEADS, HEAD_DIM)
        y_a = windowed_gqa(q, k, v, attn_sink[l]) @ w_attn_o[l]

        ug = u.astype(jnp.float32).reshape(b_, s_, SSM_GROUPS, SSM_GROUP)
        y_fwd = s5_direction(ug, ssm_a_re[l, 0], ssm_a_im[l, 0], ssm_log_step[l, 0],
                             ssm_b_re[l, 0], ssm_b_im[l, 0], ssm_c_re[l, 0], ssm_c_im[l, 0], False)
        y_bwd = s5_direction(ug, ssm_a_re[l, 1], ssm_a_im[l, 1], ssm_log_step[l, 1],
                             ssm_b_re[l, 1], ssm_b_im[l, 1], ssm_c_re[l, 1], ssm_c_im[l, 1], True)
        y_ssm = (y_fwd + y_bwd).reshape(b_, s_, SSM_WIDTH) + ssm_d[l] * ug.reshape(b_, s_, SSM_WIDTH)
        y_act = jax.nn.gelu(y_ssm, approximate=False)
        y_b = (y_act @ glu_w_a[l]) * jax.nn.sigmoid(y_act @ glu_w_b[l])

        merged = jax.nn.sigmoid(gate_a) * y_a + jax.nn.sigmoid(gate_b) * y_b
        x = x + merged @ w_out[l]

        h2 = rms_norm(x, ffn_norm_g[l])
        x = x + peer(h2, peer_w_query[l], peer_sub_keys_1[l], peer_sub_keys_2[l],
                     peer_down[l], peer_up[l])
    return x


DEPTH_2 = 2

GRID_W = 64
CTX_LEN = 256
Q_BLOCK = 128
ROPE_THETA = 10000.0
EPS = 1e-6
ALPHA = (2 * DEPTH_2) ** 0.25
BETA = (8 * DEPTH_2) ** -0.25
N_EVEN = (DEPTH_2 + 1) // 2
N_ODD = DEPTH_2 // 2

CONV_WIDTH = D_MODEL // 2
CONV_SIZE = 3
MLA_HEADS = D_MODEL // 256
MLA_Q_RANK = 512
MLA_KV_RANK = 512
MLA_NOPE = 128
MLA_ROPE = 64
MLA_V = 128
MIX_EVEN = CONV_WIDTH + MLA_HEADS * MLA_V
EVEN_IN = 3 * CONV_WIDTH + MLA_Q_RANK + MLA_KV_RANK + MLA_ROPE + MIX_EVEN
GQA_HEAD_DIM = 128
GQA_HEADS = D_MODEL // GQA_HEAD_DIM
GQA_KV_HEADS = GQA_HEADS // 4
GQA_GROUP = GQA_HEADS // GQA_KV_HEADS
MIX_ODD = GQA_HEADS * GQA_HEAD_DIM
ODD_IN = MIX_ODD + 2 * GQA_KV_HEADS * GQA_HEAD_DIM + MIX_ODD


def _rms(x, g):
    xf = x.astype(jnp.float32)
    y = xf * lax.rsqrt(jnp.mean(xf * xf, axis=-1, keepdims=True) + EPS)
    return (y * g.astype(jnp.float32)).astype(x.dtype)

def _post_norm(x, y, g, b):
    z = ALPHA * x.astype(jnp.float32) + y.astype(jnp.float32)
    mu = jnp.mean(z, axis=-1, keepdims=True)
    var = jnp.mean(jnp.square(z - mu), axis=-1, keepdims=True)
    zn = (z - mu) * lax.rsqrt(var + EPS)
    return (zn * g.astype(jnp.float32) + b.astype(jnp.float32)).astype(x.dtype)

def _rope_1d(x, pos):
    half = x.shape[-1] // 2
    inv = ROPE_THETA ** (-jnp.arange(half, dtype=jnp.float32) / half)
    ang = pos[:, None] * inv[None, :]
    cos = jnp.cos(ang)[:, None, :]
    sin = jnp.sin(ang)[:, None, :]
    xf = x.astype(jnp.float32)
    x1, x2 = xf[..., :half], xf[..., half:]
    return jnp.concatenate([x1 * cos - x2 * sin, x1 * sin + x2 * cos], axis=-1).astype(x.dtype)

def _rope_2d(x, pos_row, pos_col):
    d = x.shape[-1] // 2
    return jnp.concatenate([_rope_1d(x[..., :d], pos_row), _rope_1d(x[..., d:], pos_col)], axis=-1)

def _short_conv(u, w):
    up = jnp.pad(u, ((0, 0), (1, 1), (0, 0)))
    return up[:, :-2] * w[0] + up[:, 1:-1] * w[1] + up[:, 2:] * w[2]

def _attend(q, k, v):
    bsz, n, hk, g, dq = q.shape
    nb = n // Q_BLOCK
    scale = dq ** -0.5
    qb = q.reshape(bsz, nb, Q_BLOCK, hk, g, dq).transpose(1, 0, 2, 3, 4, 5)

    def one_block(qi):
        s = jnp.einsum('bqhgd,bkhd->bhgqk', qi, k).astype(jnp.float32) * scale
        p = jax.nn.softmax(s, axis=-1).astype(v.dtype)
        return jnp.einsum('bhgqk,bkhd->bqhgd', p, v)

    o = lax.map(one_block, qb)
    return o.transpose(1, 0, 2, 3, 4, 5).reshape(bsz, n, hk * g * v.shape[-1])

def _even_mixer(h, hc, w_in, conv_w, q_norm, w_qb, kv_norm, w_kvb, w_out, pos, need_ctx):
    o_c = 3 * CONV_WIDTH
    o_q = o_c + MLA_Q_RANK
    o_kv = o_q + MLA_KV_RANK + MLA_ROPE

    def kv_heads(kvp, rpos):
        bsz, m, _ = kvp.shape
        kv = (_rms(kvp[..., :MLA_KV_RANK], kv_norm) @ w_kvb).reshape(bsz, m, MLA_HEADS, MLA_NOPE + MLA_V)
        k_rope = kvp[..., MLA_KV_RANK:][:, :, None, :]
        if rpos is not None:
            k_rope = _rope_2d(k_rope, *rpos)
        k_rope = jnp.broadcast_to(k_rope, (bsz, m, MLA_HEADS, MLA_ROPE))
        return jnp.concatenate([kv[..., :MLA_NOPE], k_rope], axis=-1), kv[..., MLA_NOPE:]

    def q_heads(qp, rpos):
        bsz, m, _ = qp.shape
        q = (_rms(qp, q_norm) @ w_qb).reshape(bsz, m, MLA_HEADS, MLA_NOPE + MLA_ROPE)
        q_rope = q[..., MLA_NOPE:]
        if rpos is not None:
            q_rope = _rope_2d(q_rope, *rpos)
        return jnp.concatenate([q[..., :MLA_NOPE], q_rope], axis=-1)[:, :, :, None, :]

    def branch(p, attn):
        cb = p[..., :CONV_WIDTH]
        cc = p[..., CONV_WIDTH:2 * CONV_WIDTH]
        cu = p[..., 2 * CONV_WIDTH:o_c]
        conv = cb * _short_conv(cc * cu, conv_w)
        gate = jax.nn.silu(p[..., o_kv:])
        return (jnp.concatenate([conv, attn], axis=-1) * gate) @ w_out

    p = h @ w_in
    k_l, v_l = kv_heads(p[..., o_q:o_kv], pos)
    if need_ctx:
        pc = hc @ w_in
        kvc = pc[..., o_q:o_kv]
    else:
        kvc = hc @ w_in[:, o_q:o_kv]
    k_c, v_c = kv_heads(kvc, None)
    k = jnp.concatenate([k_l, k_c], axis=1)
    v = jnp.concatenate([v_l, v_c], axis=1)
    y = branch(p, _attend(q_heads(p[..., o_c:o_q], pos), k, v))
    y_ctx = branch(pc, _attend(q_heads(pc[..., o_c:o_q], None), k_c, v_c)) if need_ctx else None
    return y, y_ctx

def _odd_mixer(h, hc, w_in, q_norm, k_norm, w_out, pos, need_ctx):
    o_q = MIX_ODD
    o_k = o_q + GQA_KV_HEADS * GQA_HEAD_DIM
    o_v = o_k + GQA_KV_HEADS * GQA_HEAD_DIM

    def kv_of(kvp, rpos):
        bsz, m, _ = kvp.shape
        k = _rms(kvp[..., :o_k - o_q].reshape(bsz, m, GQA_KV_HEADS, GQA_HEAD_DIM), k_norm)
        v = kvp[..., o_k - o_q:].reshape(bsz, m, GQA_KV_HEADS, GQA_HEAD_DIM)
        if rpos is not None:
            k = _rope_2d(k, *rpos)
        return k, v

    def q_of(qp, rpos):
        bsz, m, _ = qp.shape
        q = _rms(qp.reshape(bsz, m, GQA_HEADS, GQA_HEAD_DIM), q_norm)
        if rpos is not None:
            q = _rope_2d(q, *rpos)
        return q.reshape(bsz, m, GQA_KV_HEADS, GQA_GROUP, GQA_HEAD_DIM)

    def branch(p, attn):
        return (attn * jax.nn.silu(p[..., o_v:])) @ w_out

    p = h @ w_in
    k_l, v_l = kv_of(p[..., o_q:o_v], pos)
    if need_ctx:
        pc = hc @ w_in
        kvc = pc[..., o_q:o_v]
    else:
        kvc = hc @ w_in[:, o_q:o_v]
    k_c, v_c = kv_of(kvc, None)
    k = jnp.concatenate([k_l, k_c], axis=1)
    v = jnp.concatenate([v_l, v_c], axis=1)
    y = branch(p, _attend(q_of(p[..., :o_q], pos), k, v))
    y_ctx = branch(pc, _attend(q_of(pc[..., :o_q], None), k_c, v_c)) if need_ctx else None
    return y, y_ctx

def second_inputs(seed: int = 0) -> dict:
    key = jax.random.key(seed)
    ks = jax.random.split(key, 24)
    f32 = jnp.float32

    def nrm(k, shape, scale):
        return jax.random.normal(k, shape, f32) * scale

    def gain(k, shape):
        return 1.0 + 0.02 * jax.random.normal(k, shape, f32)

    return {
        'x': nrm(ks[0], (BATCH, SEQ, D_MODEL), 1.0),
        'c': nrm(ks[1], (BATCH, D_MODEL), 1.0),
        'ctx': nrm(ks[2], (BATCH, CTX_LEN, D_MODEL), 1.0),
        'c_ctx': nrm(ks[3], (D_MODEL,), 1.0),
        'w_mod': nrm(ks[4], (DEPTH_2, D_MODEL, 3 * D_MODEL), 0.5 * D_MODEL ** -0.5),
        'b_mod': nrm(ks[5], (DEPTH_2, 3 * D_MODEL), 0.01),
        'ln_g': gain(ks[6], (DEPTH_2, D_MODEL)),
        'ln_b': nrm(ks[7], (DEPTH_2, D_MODEL), 0.02),
        'a_w_in': nrm(ks[8], (N_EVEN, D_MODEL, EVEN_IN), D_MODEL ** -0.5),
        'a_conv_w': nrm(ks[9], (N_EVEN, CONV_SIZE, CONV_WIDTH), CONV_SIZE ** -0.5),
        'a_q_norm': gain(ks[10], (N_EVEN, MLA_Q_RANK)),
        'a_w_qb': nrm(ks[11], (N_EVEN, MLA_Q_RANK, MLA_HEADS * (MLA_NOPE + MLA_ROPE)), MLA_Q_RANK ** -0.5),
        'a_kv_norm': gain(ks[12], (N_EVEN, MLA_KV_RANK)),
        'a_w_kvb': nrm(ks[13], (N_EVEN, MLA_KV_RANK, MLA_HEADS * (MLA_NOPE + MLA_V)), MLA_KV_RANK ** -0.5),
        'a_w_out': nrm(ks[14], (N_EVEN, MIX_EVEN, D_MODEL), BETA * MIX_EVEN ** -0.5),
        'c_w_in': nrm(ks[15], (N_ODD, D_MODEL, ODD_IN), D_MODEL ** -0.5),
        'c_q_norm': gain(ks[16], (N_ODD, GQA_HEAD_DIM)),
        'c_k_norm': gain(ks[17], (N_ODD, GQA_HEAD_DIM)),
        'c_w_out': nrm(ks[18], (N_ODD, MIX_ODD, D_MODEL), BETA * MIX_ODD ** -0.5),
    }

def second_block(x, c, ctx, c_ctx, w_mod, b_mod, ln_g, ln_b, a_w_in, a_conv_w, a_q_norm, a_w_qb,
              a_kv_norm, a_w_kvb, a_w_out, c_w_in, c_q_norm, c_k_norm, c_w_out):
    n = x.shape[1]
    rows = n // GRID_W
    pos_row = jnp.broadcast_to(jnp.arange(rows)[:, None], (rows, GRID_W)).reshape(-1).astype(jnp.float32)
    pos_col = jnp.broadcast_to(jnp.arange(GRID_W)[None, :], (rows, GRID_W)).reshape(-1).astype(jnp.float32)
    pos = (pos_row, pos_col)

    s_lat = jax.nn.silu(c)
    s_ctx = jax.nn.silu(c_ctx)
    h_ctx = ctx
    for layer in range(DEPTH_2):
        last = layer == DEPTH_2 - 1
        shift, scale, gate = jnp.split(s_lat @ w_mod[layer] + b_mod[layer], 3, axis=-1)
        shift_c, scale_c, gate_c = jnp.split(s_ctx @ w_mod[layer] + b_mod[layer], 3, axis=-1)
        x_in = x * (1.0 + scale[:, None, :]) + shift[:, None, :]
        c_in = h_ctx * (1.0 + scale_c) + shift_c
        if layer % 2 == 0:
            i = layer // 2
            y, y_ctx = _even_mixer(x_in, c_in, a_w_in[i], a_conv_w[i], a_q_norm[i], a_w_qb[i],
                                   a_kv_norm[i], a_w_kvb[i], a_w_out[i], pos, not last)
        else:
            i = layer // 2
            y, y_ctx = _odd_mixer(x_in, c_in, c_w_in[i], c_q_norm[i], c_k_norm[i], c_w_out[i], pos, not last)
        x = _post_norm(x, gate[:, None, :] * y, ln_g[layer], ln_b[layer])
        if not last:
            h_ctx = _post_norm(h_ctx, gate_c * y_ctx, ln_g[layer], ln_b[layer])
    return x


def setup_inputs(seed=0):
    out = dict(first_inputs(seed))
    for name, value in second_inputs(seed + 1).items():
        if name != "x":
            out[name + "_2"] = value
    return out


def reference(
    x, mix_norm_g, w_in, q_norm_g, k_norm_g, attn_sink, w_attn_o, ssm_a_re, ssm_a_im,
    ssm_log_step, ssm_b_re, ssm_b_im, ssm_c_re, ssm_c_im, ssm_d, glu_w_a, glu_w_b, w_out,
    ffn_norm_g, peer_w_query, peer_sub_keys_1, peer_sub_keys_2, peer_down, peer_up, c_2, ctx_2,
    c_ctx_2, w_mod_2, b_mod_2, ln_g_2, ln_b_2, a_w_in_2, a_conv_w_2, a_q_norm_2, a_w_qb_2,
    a_kv_norm_2, a_w_kvb_2, a_w_out_2, c_w_in_2, c_q_norm_2, c_k_norm_2, c_w_out_2,
):
    x = first_block(
        x, mix_norm_g, w_in, q_norm_g, k_norm_g, attn_sink, w_attn_o, ssm_a_re, ssm_a_im,
        ssm_log_step, ssm_b_re, ssm_b_im, ssm_c_re, ssm_c_im, ssm_d, glu_w_a, glu_w_b, w_out,
        ffn_norm_g, peer_w_query, peer_sub_keys_1, peer_sub_keys_2, peer_down, peer_up,
    )
    return second_block(
        x, c_2, ctx_2, c_ctx_2, w_mod_2, b_mod_2, ln_g_2, ln_b_2, a_w_in_2, a_conv_w_2,
        a_q_norm_2, a_w_qb_2, a_kv_norm_2, a_w_kvb_2, a_w_out_2, c_w_in_2, c_q_norm_2,
        c_k_norm_2, c_w_out_2,
    )


_drawn_inputs = setup_inputs


def setup_inputs(seed=0):
    import zlib

    import numpy as np

    out = dict(_drawn_inputs(seed))
    spreads = {}
    factors = {'mix_norm_g': 4.524,
     'q_norm_g': 8.0,
     'k_norm_g': 8.0,
     'attn_sink': 5.251,
     'ssm_a_re': 8.0,
     'ssm_b_re': 3.213,
     'ssm_b_im': 3.174,
     'ssm_c_re': 3.206,
     'ssm_c_im': 3.2,
     'ffn_norm_g': 3.051,
     'ctx_2': 8.0,
     'c_ctx_2': 4.546,
     'b_mod_2': 8.0,
     'a_q_norm_2': 8.0,
     'a_w_qb_2': 8.0,
     'a_kv_norm_2': 8.0,
     'a_w_kvb_2': 4.862,
     'c_w_in_2': 3.08,
     'c_q_norm_2': 8.0,
     'c_k_norm_2': 8.0,
     'c_w_out_2': 2.977}
    for name, (base, spread) in spreads.items():
        noise = np.random.default_rng([zlib.crc32(name.encode()), seed]).standard_normal(out[name].shape)
        drawn = base * np.exp(spread * noise) if base else spread * noise
        out[name] = __import__('jax').numpy.asarray(drawn.astype(out[name].dtype))
    for name, factor in factors.items():
        out[name] = (out[name] * factor).astype(out[name].dtype)
    return out
```

```python
from contextlib import ExitStack

import concourse.bass as bass
from concourse import mybir
import numpy as np

F32 = mybir.dt.float32
F32R = mybir.dt.float32r
U32 = mybir.dt.uint32
ALU = mybir.AluOpType
ACT = mybir.ActivationFunctionType
AX = mybir.AxisListType.X

P = 128
T = 256
D = 2048
KC = D // P
RING = 4
BLK = 16
HEADS, KVH, GROUP = 16, 4, 4
EPS = 1e-6
TOPK = 16
PH = 8
SELECT = 3
MLAH = 8
ALPHA = float(4 ** 0.25)
TURN = 6.283185
MAGIC = 12582912.0
NEG = -1e30
LOWEST = -3.4e38

PHASES = [("q", 16), ("k", 4), ("u", 8), ("v", 4), ("gate", 32), ("ssm", 64), ("glu", 16),
          ("wout", 16), ("wq", 16),
          ("down0a", 96), ("down0b", 16), ("up0", 64), ("down1", 64), ("up1", 64),
          ("lat", 9), ("conv", 32), ("agate", 8), ("mla0", 4), ("mla1", 3), ("aout", 16),
          ("k1", 4), ("v1", 4), ("q1", 16), ("attn1", 16), ("cout", 16)]
MIXED = {"ssm": [True, False, False, False], "down0a": [True, False] * 4}
G0, N0, A0 = {}, {}, {}
_g = _n = _a = 0
DENSE_AT = []
for _name, _c in PHASES:
    G0[_name], N0[_name], A0[_name] = _g, _n, _a
    _pat = MIXED.get(_name, [True])
    for _t in range(_c):
        if _pat[_t % len(_pat)]:
            DENSE_AT.append(_g)
            _n += 1
            if not _name.startswith("up"):
                _a += 4 if _name.startswith("mla") else 1
        _g += 1
NTILES, NDENSE = _g, _n

VEC, _v = {}, 0
for _name, _c in [("mix_g", 16), ("qg", 1), ("kg", 1), ("sink", 16), ("ffn_g", 16), ("ssm_re", 64),
                  ("ssm_im", 64), ("ssm_ls", 64), ("ssm_d", 8), ("cvec", 32), ("bmod", 96),
                  ("lng", 32), ("lnb", 32), ("convw", 24), ("aqn", 4), ("akvn", 4), ("cqn", 1),
                  ("ckn", 1), ("slope", 16), ("eps", 1), ("halfpi", 1), ("tab", 32)]:
    VEC[_name] = (_v, _c)
    _v += _c
NVEC = (_v + 7) // 8 * 8
CONST = {}
_v = 0
for _name, _c in [("ident", 128), ("ones", 128), ("iota", 128), ("nd", 512), ("rm", 1024),
                  ("rg", 512), ("perm_m", 128), ("perm_g", 128)]:
    CONST[_name] = (_v, _c)
    _v += _c
NCONST = _v


def at(c, i, s):
    return c if i is None or s == 0 else i * s + c


class Tile:

    def __init__(self, phase, j, i=None, per=0, dper=None, acc=1, skip=0):
        self.i, self.gs = i, per
        self.ns = per if dper is None else dper
        g0 = G0[phase] + j + skip
        self.slot, self.g0 = g0 % RING, g0
        pat = MIXED.get(phase, [True])
        jd = sum(pat[t % len(pat)] for t in range(j + skip))
        self.n0 = N0[phase] + jd
        self.par = self.n0 % 2
        self.a0 = A0[phase] + (4 * jd if phase.startswith("mla") else jd)

    def loaded(self):
        return at(16 * (self.g0 // RING + 1), self.i, 16 * self.gs // RING)

    def done(self):
        return at(self.g0 + 1, self.i, self.gs)

    def bank(self):
        return self.a0 % 4

    def bank_free(self):
        return at(self.a0 // 4 + 1, self.i, self.ns // 4)

    def next(self):
        t = Tile.__new__(Tile)
        t.i, t.gs, t.ns, t.n0 = self.i, self.gs, self.ns, self.n0 + 1
        t.g0 = DENSE_AT[t.n0] if t.n0 < NDENSE else None
        t.slot = t.g0 % RING if t.g0 is not None else None
        t.par = t.n0 % 2
        return t


class Sig:

    def __init__(self, eng, sem):
        self.eng, self.sem, self.n, self.i, self.per, self.start = eng, sem, 0, None, 0, 0

    def inc(self, ins):
        ins.then_inc(self.sem, 1)
        self.n += 1
        return ins

    def now(self):
        return at(self.n, self.i, self.per)

    def link(self, ins):
        self.inc(ins)
        self.eng.wait_ge(self.sem, self.now())


class Loop:

    def __init__(self, eng, times, sigs):
        self.eng, self.times, self.sigs = eng, times, sigs

    def __enter__(self):
        self.f = self.eng.Fori(0, self.times, 1)
        i = self.f.__enter__()
        for s, per in self.sigs.items():
            s.i, s.per, s.start = i, per, s.n
        return i

    def __exit__(self, *a):
        if a[0] is None:
            for s, per in self.sigs.items():
                assert s.n - s.start == per, (s.sem, s.n - s.start, per)
                s.n, s.i = s.start + per * self.times, None
        return self.f.__exit__(*a)


def build(nc, stream, vecs, consts, x_in, ctx_in, ssm_b, ssm_c, subkeys, out):
    es = ExitStack()
    with es:
        base = (nc.sbuf_base + 31) // 32 * 32
        top = nc.sbuf_usable_end
        mem = {}

        def place(name, shape, dt, off):
            n = int(np.prod(shape[1:])) * 4
            assert base + off + n <= top, (name, off + n, top - base)
            mem[name] = nc.alloc_sbuf_tensor_at(name, shape, dt, offset=base + off)
            return mem[name]

        K = 1024
        ring = place("ring", [P, RING, BLK, P], F32, 0)
        w_hi = place("w_hi", [P, 2, BLK, P], F32R, 32 * K)
        w_lo = place("w_lo", [P, 2, BLK, P], F32R, 48 * K)
        vec = place("vec", [P, NVEC], F32, 64 * K)
        cst = place("cst", [P, NCONST], F32, 64 * K + NVEC * 4)
        o = (64 * K + NVEC * 4 + NCONST * 4 + 31) // 32 * 32
        small = place("small", [P, 448], F32, o)
        mods = place("mods", [P, 2, 48, 2], F32, o + 1792)
        Dd = o + 1792 + 768
        X = place("X", [P, KC, T], F32, Dd)
        h_hi = place("h_hi", [P, KC, T], F32R, Dd + 16 * K)
        h_lo = place("h_lo", [P, KC, T], F32R, Dd + 32 * K)
        qku = place("qku", [P, 28, T], F32, Dd + 48 * K)
        v_tok = place("v_tok", [P, 2, 512], F32, Dd + 76 * K)
        gates = place("gates", [P, 32, T], F32, Dd + 80 * K)
        TA = Dd + 112 * K
        sq = place("sq", [P, 2, 4, T], F32, TA)
        rs = place("rs", [P, 2, T], F32, TA + 8 * K)
        ht = place("ht", [P, KC, T], F32, Dd + 80 * K)
        sq5 = place("sq5", [P, 5, T], F32, TA)
        rq5 = place("rq5", [P, 5, T], F32, TA + 5 * K)
        v_grp = place("v_grp", [P, 2, P], F32, TA + 10 * K)
        sco = place("sco", [P, 2, T], F32, TA + 11 * K)
        prt = place("prt", [P, 2, T], F32, TA + 13 * K)
        st = small[:, 16:32]
        cs = small[:, 32:64].rearrange("p (k s) -> p k s", s=2)
        s5_r, s5_fh, s5_fl, s5_kr, s5_ki = (small[:, 64 + 64 * n:128 + 64 * n] for n in range(5))
        s5w = place("s5w", [P, 14, 64], F32, TA + 10 * K)
        SS = Dd + 48 * K
        b_st = place("b_st", [P, 2, 2, 2, P], F32, SS)
        c_st = place("c_st", [P, 2, 8, 32], F32, SS + 4 * K)
        c_out = place("c_out", [P, 2, 8, 3, 32], F32, SS + 6 * K)
        ph = place("ph", [P, 3, 8, 32], F32, SS + 12 * K)
        phs = place("phs", [P, 2, 8, 32], F32, SS + 15 * K)
        uc = place("uc", [P, 2, T], F32, SS + 17 * K)
        us2 = place("us2", [P, T], F32, SS + 19 * K)
        tab = place("tab", [P, 2, 2, 8, 32], F32, Dd + 76 * K)
        rot = place("rot", [P, 2, 2, 16, 16], F32, TA)
        _nd = CONST["nd"][0]
        rt = cst[:, _nd:_nd + 512].rearrange("p (a b c) -> p a b c", a=2, b=16)
        td = place("td", [P, 2, 2, T], F32, TA + 4 * K)
        pq = place("pq", [P, 2, 2, 2, T], F32, TA + 8 * K)
        sg = place("sg", [P, 2, 512], F32, TA)
        HE = P // 2
        ab = place("ab", [P, HE, T], F32, Dd + 48 * K)
        sk = place("sk", [P, 16, P], F32, Dd + 48 * K)
        kt = place("kt", [P, 3, T], F32, TA)
        ix = place("ix", [P, 2, 3, P], F32, TA + 3 * K)
        sv = place("sv", [P, 2, PH, TOPK], F32, TA + 6 * K)
        qs = place("qs", [P, 4, T], F32, TA + 7 * K)
        tv = place("tv", [P, 2, 16, TOPK], F32, TA + 11 * K)
        ti = place("ti", [P, 2, 16, TOPK], F32, TA + 13 * K)
        vv = place("vv", [P, 4, 2, TOPK], F32, TA + 15 * K)
        ii = place("ii", [P, 4, 2, TOPK], U32, TA + 15 * K + 512)
        mt = place("mt", [P, P], F32, TA + 16 * K)
        cand = place("cand", [P, TOPK, TOPK], F32, TA + 7 * K)
        cand2 = place("cand2", [P, TOPK, TOPK], F32, TA + 8 * K)
        eq = place("eq", [P, 2, TOPK, TOPK], F32, TA + 9 * K)
        oh2 = place("oh2", [P, 2, 8, P], F32, TA + 3 * K)
        oh1 = place("oh1", [P, 2, 8, HE], F32, TA + 11 * K)
        wp_hi = place("wp_hi", [P, 2, T], F32R, TA + 3 * K)
        wp_lo = place("wp_lo", [P, 2, T], F32R, TA + 5 * K)
        N2 = 2 * T
        xc = place("xc", [P, KC, T], F32, Dd + 16 * K)
        h2_hi = place("h2_hi", [P, KC, N2], F32R, Dd + 32 * K)
        h2_lo = place("h2_lo", [P, KC, N2], F32R, Dd + 64 * K)
        hm = place("hm", [P, KC, N2], F32, Dd + 96 * K)
        mx = place("mx", [P, KC, N2], F32, Dd + 96 * K)
        XX = place("XX", [P, KC, N2], F32, Dd)
        lat = place("lat", [P, 8, N2], F32, Dd)
        rk = place("rk", [P, N2], F32, Dd + 16 * K)
        CT = Dd + 18 * K
        lsq = place("lsq", [P, 2, N2], F32, CT)
        lrt = place("lrt", [P, 2, N2], F32, CT + 4 * K)
        cvc = place("cvc", [P, N2], F32, CT + 8 * K)
        cvu = place("cvu", [P, 2, T + 8], F32, CT + 10 * K)
        cva = place("cva", [P, N2], F32, CT)
        cvg = place("cvg", [P, N2], F32, CT + 2 * K)
        lh = place("lh", [P, 8, N2], F32R, Dd + 32 * K)
        ll = place("ll", [P, 8, N2], F32R, Dd + 48 * K)
        qn = place("qn", [P, 4, N2], F32, Dd + 64 * K)
        kn = place("kn", [P, 4, N2], F32, Dd + 72 * K)
        vn = place("vn", [P, 4, N2], F32, Dd + 80 * K)
        mrt = place("mrt", [P, 2, N2], F32, Dd + 88 * K)
        mst = place("mst", [P, 2, 16], F32, Dd + 92 * K)
        qr = place("qr", [P, 4, N2], F32, Dd)
        msc = place("msc", [P, 3, N2], F32, Dd + 8 * K)
        mpt = place("mpt", [P, 3, N2], F32, CT)
        lnm = place("lnm", [P, N2], F32, Dd + 112 * K)
        lnr = place("lnr", [P, 2, N2], F32, Dd + 114 * K)
        lns = place("lns", [P, 2, 4, N2], F32, Dd + 96 * K)
        k1 = place("k1", [P, KVH, N2], F32, Dd + 96 * K)
        v1 = place("v1", [P, 4, N2], F32, Dd + 104 * K)
        q1 = place("q1", [P, HEADS, T], F32, Dd + 112 * K)
        x_save = nc.dram_tensor("x_save", [P, KC, T], F32).ap()

        def xt(a, n=1):
            return XX[:, a:a + n, T:N2]

        def x_tok(x, k, tt):
            return x[:, k, tt * P:(tt + 1) * P]

        def md(layer, part, k, seq):
            return mods[:, layer, 16 * part + k, seq:seq + 1]

        def mdd(layer, part, k, seq):
            return mods[:, layer, bass.ds(k + 16 * part, 1), seq]

        def V(name, c=0, n=1):
            a = VEC[name][0] + c
            return vec[:, a:a + n]

        def Vd(name, c):
            return vec[:, bass.ds(c + VEC[name][0], 1)]

        def C(name, a=0, b=None):
            s, n = CONST[name]
            return cst[:, s + a:s + (n if b is None else b)]

        banks = es.enter_context(nc.psum_tensor("banks", [P, 8, 512], F32))

        def bank(b, n=512, a=0):
            return banks[:, b, a:a + n]

        sems = {}

        def S(name):
            if name not in sems:
                sems[name] = es.enter_context(nc.semaphore(name))
            return sems[name]

        tile_loaded = [S(f"tile_loaded{r}") for r in range(RING)]
        lo_done = [S("lo_done_pool"), S("lo_done_dve")]
        hi_done, mm_done = S("hi_done"), S("mm_done")
        acc_free = [S(f"acc_free{b}") for b in range(4)]
        HALF = BLK // 2

        def hi_split(act, t):
            if t.g0 is None:
                return
            act.wait_ge(tile_loaded[t.slot], t.loaded())
            if t.n0 >= 2:
                act.wait_ge(mm_done, at(DENSE_AT[t.n0 - 2] + 1, t.i, t.gs))
            for h in range(2):
                s = slice(h * HALF, (h + 1) * HALF)
                act.copy(w_hi[:, t.par, s], ring[:, t.slot, s]).then_inc(hi_done, 1)

        def lo_split(eng, t, h):
            if t.g0 is None:
                return
            eng.wait_ge(hi_done, at(2 * t.n0 + 2 - h, t.i, 2 * t.ns))
            s = slice((1 - h) * HALF, (2 - h) * HALF)
            eng.tensor_tensor(w_lo[:, t.par, s], ring[:, t.slot, s], w_hi[:, t.par, s].bitcast(F32),
                              ALU.subtract).then_inc(lo_done[h], 1)

        def wait_weights(pe, t):
            for h in range(2):
                pe.wait_ge(lo_done[h], at(t.n0 + 1, t.i, t.ns))

        def dense(pe, t, xh, xl, n=T, b=None):
            b = t.bank() if b is None else b
            pe.wait_ge(acc_free[b], t.bank_free())
            pe.wait_ge(lo_done[1], at(t.n0 + 1, t.i, t.ns))
            for k in range(BLK):
                if k == HALF:
                    pe.wait_ge(lo_done[0], at(t.n0 + 1, t.i, t.ns))
                for w, x in ((w_hi, xh), (w_lo, xh), (w_hi, xl)):
                    m = pe.matmul(bank(b, n), w[:, t.par, k], x(k), start=(k == 0 and w is w_hi and x is xh),
                                  stop=(k == BLK - 1 and x is xl))
            m.then_inc(mm_done, 1)

        def xh1(k): return h_hi[:, k]
        def xl1(k): return h_lo[:, k]

        block = es.enter_context(nc.Block())

        @block.sync
        def _(sp):
            for r in range(RING):
                sp.dma_start(ring[:, r], stream[r]).then_inc(tile_loaded[r], 16)
            with sp.Fori(1, NTILES // RING, 1) as i:
                for r in range(RING):
                    sp.wait_ge(mm_done, (i - 1) * RING + (r + 1))
                    sp.dma_start(ring[:, r], stream[i * RING + r]).then_inc(tile_loaded[r], 16)
            for g in range(NTILES // RING * RING, NTILES):
                sp.wait_ge(mm_done, g - RING + 1)
                sp.dma_start(ring[:, g % RING], stream[g]).then_inc(tile_loaded[g % RING], 16)

        @block.scalar
        def _(act):
            chain = Sig(act, S("act_chain"))
            act.dma_start(vec[:], vecs).then_inc(S("in_ready"), 16)
            act.dma_start(cst[:], consts).then_inc(S("in_ready"), 16)
            act.dma_start(X[:], x_in).then_inc(S("in_ready"), 16)
            act.wait_ge(S("in_ready"), 48)
            hi_split(act, Tile("q", 0))
            act.activation(cs[:], V("cvec", 0, 32).rearrange("p (k s) -> p k s", s=2), ACT.Silu)\
                .then_inc(S("cs_ready"), 1)
            act.activation(s5w[:, 0], V("ssm_ls", 0, 64), ACT.Exp).then_inc(S("s5_act"), 1)
            act.wait_ge(S("s5_dve"), 1)
            act.activation(s5_r, s5w[:, 1], ACT.Exp).then_inc(S("s5_act"), 1)
            act.activation(s5w[:, 6:8], s5w[:, 4:6], ACT.Sin, scale=TURN).then_inc(S("s5_act"), 1)

            def norm_stats(r):
                if r:
                    act.wait_ge(S("x1_ready"), 1)
                for q in range(4):
                    if q >= 2:
                        act.wait_ge(S(f"sum_done{r}"), q - 1)
                    act.activation(sq[:, q % 2], X[:, 4 * q:4 * q + 4], ACT.Square).then_inc(S(f"sq_ready{r}"), 1)
                act.wait_ge(S(f"sum_done{r}"), 4)
                act.activation(rs[:, 0], bank(6, T), ACT.Sqrt, bias=V("eps"), scale=1.0 / D)\
                    .then_inc(S(f"root{r}"), 1)

            def split_hi(src, dst, ready, done, n=4, w=4, b0=0):
                for q in range(n):
                    if ready is not None:
                        act.wait_ge(ready, q + 1 + b0)
                    act.copy(dst[:, w * q:w * q + w], src[:, w * q:w * q + w]).then_inc(done, 1)

            norm_stats(0)
            split_hi(ht, h_hi, S("ht_ready0"), S("h_hi_done0"))
            for j in range(4):
                hi_split(act, Tile("q", j).next())
            with act.Fori(0, 6, 1) as i:
                for j in range(4):
                    hi_split(act, Tile("q", j, i, 4, skip=4).next())
            for j in range(4):
                hi_split(act, Tile("v", j).next())
            act.wait_ge(S("qkuv_done"), 1)
            e_negm = S("negmax_ready")
            with Loop(act, 4, {chain: 2}) as i:
                act.wait_ge(S("scores_done"), i * 4 + 1)
                chain.inc(act.activation(sq5[:, 0], qku[:, i + 16], ACT.Square))
                act.activation(sq5[:, 1:5], qku[:, bass.ds(i * 4, 4)], ACT.Square).then_inc(S("sq5_ready"), 1)
                act.wait_ge(S("pv_done"), i * 4 + 1)
                act.copy(v_grp[:], v_tok[:, :, bass.ds(i * P, P)]).then_inc(S("vgrp_ready"), 1)
                act.wait_ge(S("norm5_done"), i + 1)
                act.activation(rq5[:, 1:5], banks[:, 4:6, :].rearrange("p a (b t) -> p (a b) t", t=T),
                               ACT.Sqrt, bias=V("eps"), scale=1.0 / P).then_inc(S("root5"), 1)
                chain.inc(act.activation(rq5[:, 0], bank(6, T), ACT.Sqrt, bias=V("eps"), scale=1.0 / P))
                for j in range(4):
                    ta, tb = Tile("gate", 2 * j, i, 8), Tile("gate", 2 * j + 1, i, 8)
                    hi_split(act, ta.next())
                    act.wait_ge(mm_done, ta.done())
                    act.activation(gates[:, i * 8 + 2 * j], bank(ta.bank(), T), ACT.Sigmoid)\
                        .then_inc(acc_free[ta.bank()], 1)
                    hi_split(act, tb.next())
                    act.wait_ge(e_negm, i * 4 + (j + 1))
                    for b in range(2):
                        act.activation(sco[:, b], sco[:, b], ACT.Exp, bias=st[:, 2 + b:3 + b],
                                       accum_out=st[:, 4 + b:5 + b])
                    act.activation(st[:, 6:8], st[:, 2:4], ACT.Exp, bias=Vd("sink", i * 4 + j))\
                        .then_inc(S("exp_done"), 1)
                    act.wait_ge(S("ptr_done"), i * 4 + (j + 1))
                    act.copy(prt[:], bank(6)).then_inc(S("prt_ready"), 1)
                    act.wait_ge(mm_done, tb.done())
                    act.activation(gates[:, i * 8 + (2 * j + 1)], bank(tb.bank(), T), ACT.Sigmoid)\
                        .then_inc(acc_free[tb.bank()], 1)

            act.wait_ge(mm_done, G0["ssm"])
            act.wait_ge(S("o_ready"), 1)
            split_hi(qku, h_hi, None, S("o_hi_done"))

            act.wait_ge(S("o_lo_done"), 4)
            act.dma_start(b_st[:, 0], ssm_b[0]).then_inc(S("b_loaded"), 16)
            act.dma_start(c_st[:], ssm_c[0]).then_inc(S("c_loaded"), 16)
            act.copy(uc[:, 0], qku[:, 20]).then_inc(S("us_ready"), 1)
            act.sem_inc(S("gelu_done"), 1)
            act.sem_inc(S("tab_ready"), 1)

            def tables(c0, i):
                act.wait_ge(S("phs_ready"), at(c0 + 1, i, 2))
                act.activation(tab[:, c0 % 2], phs[:], ACT.Sin, scale=TURN).then_inc(S("tab_ready"), 1)

            tables(0, None)

            def ssm_act(c0, i):
                c = at(c0, i, 2)
                if not (i is None and c0 == 7):
                    act.wait_ge(S("bu_done"), at(8 * c0 + 1, i, 16))
                    act.dma_start(b_st[:, 1 - c0 % 2], ssm_b[at(c0 + 1, i, 2)]).then_inc(S("b_loaded"), 16)
                    act.copy(uc[:, 1 - c0 % 2], qku[:, at(21 + c0, i, 2)]).then_inc(S("us_ready"), 1)
                    act.wait_ge(S("c_made"), at(c0 + 1, i, 2))
                    act.dma_start(c_st[:], ssm_c[at(c0 + 1, i, 2)]).then_inc(S("c_loaded"), 16)
                hi_split(act, Tile("ssm", 8 * c0, i, 16, 4).next())
                if not (i is None and c0 == 7):
                    tables(c0 + 1, i)
                hi_split(act, Tile("ssm", 8 * c0 + 4, i, 16, 4).next())
                act.wait_ge(S("y_ready"), at(c0 + 1, i, 2))
                act.copy(small[:, 8:9], small[:, 0:1])
                act.activation(qku[:, at(20 + c0, i, 2)], us2[:], ACT.Gelu).then_inc(S("gelu_done"), 1)

            with act.Fori(0, 3, 1) as i:
                ssm_act(0, i)
                ssm_act(1, i)
            ssm_act(6, None)
            ssm_act(7, None)
            act.wait_ge(mm_done, G0["glu"])
            act.wait_ge(S("gelu_done"), 9)
            for q in range(2):
                act.copy(h_hi[:, 4 * q:4 * q + 4], qku[:, 20 + 4 * q:24 + 4 * q]).then_inc(S("ya_hi_done"), 1)
            with act.Fori(0, 4, 1) as i:
                for j in range(2):
                    ta, tb = Tile("glu", 2 * j, i, 4), Tile("glu", 2 * j + 1, i, 4)
                    hi_split(act, ta.next())
                    hi_split(act, tb.next())
                    act.wait_ge(mm_done, tb.done())
                    act.wait_ge(S("glu_done"), i * 2 + (j + 1))
                    act.activation(sg[:, j], bank(tb.bank()), ACT.Sigmoid).then_inc(S("sg_ready"), 1)
            act.wait_ge(mm_done, G0["wout"])
            split_hi(gates, h_hi, S("merged_ready"), S("m_hi_done"))
            with act.Fori(0, 4, 1) as i:
                for j in range(4):
                    hi_split(act, Tile("wout", j, i, 4).next())

            act.dma_start(sk[:], subkeys).then_inc(S("sk_loaded"), 16)
            norm_stats(1)
            split_hi(ht, h_hi, S("ht_ready1"), S("h_hi_done1"))
            with act.Fori(0, 4, 1) as i:
                for j in range(4):
                    t = Tile("wq", j, i, 4)
                    hi_split(act, t.next())
                    act.wait_ge(mm_done, t.done())
                    act.wait_ge(S("qs_used"), at(j + 1, i, 4))
                    act.copy(qs[:, j], bank(t.bank(), T)).then_inc(acc_free[t.bank()], 1)

            def down_act(t, row):
                act.wait_ge(mm_done, t.done())
                act.activation(ab[:, row], bank(t.bank(), T), ACT.Gelu).then_inc(acc_free[t.bank()], 1)

            def up_act(half):
                with act.Fori(0, 16, 1) as i:
                    for j in range(4):
                        hi_split(act, Tile(f"up{half}", j, i, 4).next())

            for j in range(4 * SELECT):
                t = Tile("down0a", 2 * j)
                hi_split(act, t.next())
                down_act(t, j)
            act.wait_ge(S("sel_shifted"), 1)
            act.activation(sv[:], sv[:], ACT.Exp).then_inc(S("sel_exp"), 1)
            with act.Fori(0, 12 - SELECT, 1) as i:
                for j in range(4):
                    t = Tile("down0a", 2 * j, i, 8, 4, skip=8 * SELECT)
                    hi_split(act, t.next())
                    down_act(t, i * 4 + (j + 4 * SELECT))
            with act.Fori(0, 4, 1) as i:
                for j in range(4):
                    t = Tile("down0b", j, i, 4)
                    hi_split(act, t.next())
                    down_act(t, i * 4 + (j + 48))
            act.sem_inc(S("acts_done"), 1)
            up_act(0)
            with act.Fori(0, 16, 1) as i:
                for j in range(4):
                    t = Tile("down1", j, i, 4)
                    hi_split(act, t.next())
                    down_act(t, i * 4 + j)
            act.sem_inc(S("acts_done"), 1)
            up_act(1)

            act.wait_ge(S("spilled"), 16)
            act.dma_start(x_save, X[:]).then_inc(S("x_saved"), 16)
            act.dma_start(xc[:], ctx_in).then_inc(S("ctx_loaded"), 16)

            def mixer_in_hi(n, seqs):
                for q in range(4):
                    act.wait_ge(S("hm_ready"), q + 1 + 4 * n)
                    act.copy(h2_hi[:, 4 * q:4 * q + 4], hm[:, 4 * q:4 * q + 4]).then_inc(S("hm_hi"), 1)

            mixer_in_hi(0, 2)
            for j in range(9):
                hi_split(act, Tile("lat", j).next())
            act.wait_ge(S("lat_read"), 9)
            for k in range(8):
                if k >= 2:
                    act.wait_ge(S("lsum_done"), k - 1)
                act.activation(lsq[:, k % 2], lat[:, k], ACT.Square).then_inc(S("lsq_ready"), 1)
            for f in range(2):
                act.wait_ge(S("lsum_done"), 4 * f + 4)
                act.activation(lrt[:, f], bank(6 + f), ACT.Sqrt, bias=V("eps"), scale=1.0 / 512)\
                    .then_inc(S("lroot"), 1)
            act.wait_ge(S("lat_normed"), 1)
            with act.Fori(0, 8, 1) as i:
                tb, tc, tu, tg = (Tile("conv", j, i, 4) for j in range(4))
                hi_split(act, tb.next())
                hi_split(act, tc.next())
                act.wait_ge(mm_done, tc.done())
                act.wait_ge(S("cv_done"), at(1, i, 1))
                act.copy(cvc[:], bank(tc.bank())).then_inc(S("cvc_ready"), 1)
                hi_split(act, tu.next())
                hi_split(act, tg.next())
                act.wait_ge(mm_done, tg.done())
                act.activation(cvg[:], bank(tg.bank()), ACT.Silu).then_inc(S("cvg_ready"), 1)
            with act.Fori(0, 2, 1) as i:
                for j in range(4):
                    t = Tile("agate", j, i, 4)
                    hi_split(act, t.next())
                    act.wait_ge(mm_done, t.done())
                    act.activation(mx[:, i * 4 + (j + 8)], bank(t.bank()), ACT.Silu).then_inc(acc_free[t.bank()], 1)
            for q in range(4):
                act.copy(lh[:, 2 * q:2 * q + 2], lat[:, 2 * q:2 * q + 2]).then_inc(S("lh_done"), 1)
            for hh in range(2):
                for j in range(4 - hh):
                    t = Tile(f"mla{hh}", j)
                    hi_split(act, t.next())
                    act.wait_ge(mm_done, t.done())
                    if j == 0 and hh:
                        act.wait_ge(S("mpv_done"), 8)
                    if j in (0, 3):
                        if j == 3:
                            act.wait_ge(S("ll_done"), 4)
                        for m in range(4):
                            dst = qn if j == 0 else qr
                            act.activation(dst[:, m], bank((t.a0 + m) % 4), ACT.Copy, scale=192.0 ** -0.5)\
                                .then_inc(acc_free[(t.a0 + m) % 4], 1)
                for j in range(4):
                    n = 4 * hh + j
                    if n:
                        act.wait_ge(S("mtr_done"), n)
                    for b in range(2):
                        act.wait_ge(S("mmax_ready"), 3 * n + b + 1)
                        act.activation(msc[:, b], bank(4 + b), ACT.Exp, bias=mst[:, n % 2, b:b + 1],
                                       accum_out=mst[:, n % 2, 4 + b:5 + b]).then_inc(S("mexp_done"), 1)
                    act.wait_ge(S("mmax_ready"), 3 * n + 3)
                    for b in range(2):
                        m_ = act.activation(msc[:, 2, b * T:(b + 1) * T], bank(6, T, b * T), ACT.Exp,
                                            bias=mst[:, n % 2, 2 + b:3 + b], accum_out=mst[:, n % 2, 6 + b:7 + b])
                    m_.then_inc(S("mexp_done"), 1)
                    act.wait_ge(S("mtr_done"), n + 1)
                    for b in range(2):
                        act.copy(mpt[:, b], bank(b)).then_inc(S("mpt_act"), 1)

            def act_out(name, layer, n):
                act.wait_ge(S("mixed"), 1 + layer)
                src = mx if layer == 0 else q1
                for q in range(4):
                    act.copy(h2_hi[:, 4 * q:4 * q + 4, 0:n], src[:, 4 * q:4 * q + 4]).then_inc(S("mx_hi"), 1)
                if layer == 0:
                    act.wait_ge(S("x_saved"), 16)
                    act.dma_start(XX[:, :, 0:T], x_save).then_inc(S("xx_loaded"), 16)
                    act.dma_start(XX[:, :, T:N2], ctx_in).then_inc(S("xx_loaded"), 16)
                    act.wait_ge(S("xx_loaded"), 32)
                for q in range(4):
                    x = XX[:, 4 * q:4 * q + 4, 0:n]
                    act.activation(x, x, ACT.Copy, scale=ALPHA).then_inc(S("xx_scaled"), 1)
                with act.Fori(0, 4 if layer == 0 else 3, 1) as i:
                    for j in range(4):
                        hi_split(act, Tile(name, j, i, 4).next())
                if layer:
                    for j in range(4):
                        hi_split(act, Tile(name, 12 + j).next())
                act.wait_ge(S("ln_sum"), 1 + layer)
                act.activation(lnm[:, 0:n], bank(6, n), ACT.Copy, scale=1.0 / D).then_inc(S("ln_mean"), 1)
                for q in range(4):
                    act.wait_ge(S("ln_cent"), q + 1 + 4 * layer)
                    if q >= 2:
                        act.wait_ge(S("ln_sqsum"), q - 1 + 4 * layer)
                    act.activation(lns[:, q % 2, :, 0:n], XX[:, 4 * q:4 * q + 4, 0:n], ACT.Square)\
                        .then_inc(S("ln_sq"), 1)
                act.wait_ge(S("ln_sqsum"), 4 + 4 * layer)
                act.activation(lnr[:, 0, 0:n], bank(7, n), ACT.Sqrt, bias=V("eps"), scale=1.0 / D)\
                    .then_inc(S("ln_root"), 1)

            act_out("aout", 0, N2)
            mixer_in_hi(1, 2)
            for j in range(8):
                hi_split(act, Tile("k1", j).next())

            def head_act(j, i, t, c1, per, src, n):
                act.wait_ge(S("hraw_ready"), at(c1 + 1, i, per))
                act.activation(xt(2, 2) if n == N2 else xt(2), src, ACT.Square).then_inc(S("hsq_ready"), 1)
                act.wait_ge(S("hsum_done"), at(c1 + 1, i, per))
                act.activation(xt(4, 2) if n == N2 else xt(4), bank(4, n), ACT.Sqrt, bias=V("eps"), scale=1.0 / P)\
                    .then_inc(S("hroot"), 1)

            for j in range(4):
                head_act(j, None, None, j, 0, xt(0, 2), N2)
            with act.Fori(0, 4, 1) as i:
                for j in range(4):
                    hi_split(act, Tile("q1", j, i, 4).next())
                    head_act(j, i, None, 4 + j, 4, xt(0), T)
            with act.Fori(0, 4, 1) as i:
                act.wait_ge(S("h1pv_done"), at(1, i, 4))
                act.copy(xt(0, 2), k1[:, i].rearrange("p (a t) -> p a t", a=2)).then_inc(S("kg_ready"), 1)
                for a in range(2):
                    m_ = act.copy(XX[:, 2 + a, T:N2].rearrange("p (b d) -> p b d", b=2),
                                  v1[:, 2 * a:2 * a + 2, bass.ds(i * P, P)])
                m_.then_inc(S("vg_ready"), 1)
                for j in range(4):
                    t = Tile("attn1", j, i, 4)
                    n = lambda k: at(j + k, i, 4)
                    hi_split(act, t.next())
                    for b in range(2):
                        act.wait_ge(S("h1max_ready"), at(2 * j + b + 1, i, 8))
                        act.activation(xt(6 + 2 * b, 2), bank(4 + b).rearrange("p (a t) -> p a t", a=2), ACT.Exp,
                                       bias=st[:, b:b + 1], accum_out=st[:, 4 + b:5 + b]).then_inc(S("h1exp_done"), 1)
                    act.wait_ge(S("h1tr_done"), n(1))
                    act.copy(xt(10, 2), bank(6).rearrange("p (a t) -> p a t", a=2)).then_inc(S("h1pt_act"), 1)
                    act.wait_ge(mm_done, t.done())
                    act.activation(xt(14), bank(t.bank(), T), ACT.Silu).then_inc(S("g1_ready"), 1)
            act_out("cout", 1, T)
            act.wait_ge(S("out_ready"), 4)
            act.dma_start(out, XX[:, :, 0:T]).then_inc(S("stored"), 16)
            act.wait_ge(S("stored"), 16)

        @block.gpsimd
        def _(pool):
            lo_split(pool, Tile("q", 0), 0)
            for j in range(4):
                lo_split(pool, Tile("q", j).next(), 0)
            with pool.Fori(0, 6, 1) as i:
                for j in range(4):
                    lo_split(pool, Tile("q", j, i, 4, skip=4).next(), 0)
            for j in range(4):
                lo_split(pool, Tile("v", j).next(), 0)
            with pool.Fori(0, 4, 1) as i:
                for j in range(8):
                    lo_split(pool, Tile("gate", j, i, 8).next(), 0)


            def ssm_pool(c0, i):
                pool.wait_ge(S("tab_ready"), at(c0 + 2, i, 2))
                for v in range(8):
                    if v in (3, 7):
                        lo_split(pool, Tile("ssm", 8 * c0 + v - 3, i, 16, 4).next(), 0)
                    sa, sb_, ca, cb = (tab[:, c0 % 2, f, v, o:o + 16] for f in range(2) for o in (0, 16))
                    A_ = lambda a: a.unsqueeze(2).to_broadcast([P, 16, 16])
                    B_ = lambda a: a.unsqueeze(1).to_broadcast([P, 16, 16])
                    u = lambda n: at(8 * c0 + v + n, i, 16)
                    pool.wait_ge(S("rot_used"), u(1))
                    for f, (p0, p1, p2, p3, op) in enumerate(((ca, cb, sa, sb_, ALU.subtract),
                                                              (sa, cb, ca, sb_, ALU.add))):
                        pool.tensor_tensor(rt[:, 0], A_(p0), B_(p1), ALU.mult)
                        pool.tensor_tensor(rt[:, 1], A_(p2), B_(p3), ALU.mult).then_inc(S("rt_ready"), 1)
                        pool.wait_ge(S("rt_ready"), at(2 * (8 * c0 + v) + f + 1, i, 32))
                        pool.tensor_tensor(rot[:, v % 2, f], rt[:, 0], rt[:, 1], op).then_inc(S("rot_ready"), 1)
                        pool.wait_ge(S("rot_ready"), at(2 * (8 * c0 + v) + f + 1, i, 32))

            with pool.Fori(0, 3, 1) as i:
                ssm_pool(0, i)
                ssm_pool(1, i)
            ssm_pool(6, None)
            ssm_pool(7, None)
            for ph_, cnt in (("glu", 4), ("wout", 4)):
                with pool.Fori(0, cnt, 1) as i:
                    for j in range(4):
                        lo_split(pool, Tile(ph_, j, i, 4).next(), 0)

            with pool.Fori(0, 4, 1) as i:
                for j in range(4):
                    lo_split(pool, Tile("wq", j, i, 4).next(), 0)
            pool.wait_ge(lo_done[1], N0["down0a"] + 1)
            for j in range(4 * SELECT):
                for h in (1, 0):
                    lo_split(pool, Tile("down0a", 2 * j).next(), h)
            with pool.Fori(0, 12 - SELECT, 1) as i:
                for j in range(4):
                    lo_split(pool, Tile("down0a", 2 * j, i, 8, 4, skip=8 * SELECT).next(), 0)
            with pool.Fori(0, 4, 1) as i:
                for j in range(4):
                    lo_split(pool, Tile("down0b", j, i, 4).next(), 0)

            def gates_pool(half):
                if half == 0:
                    pool.wait_ge(S("kt_ready"), 1)
                else:
                    pool.wait_ge(S("spilled"), 8)
                with pool.Fori(0, 16, 1) as i:
                    for j in range(2):
                        b0 = lambda n: at(2 * 16 * half + j + n, i, 2)
                        ts = bass.ds(i * 16 + 8 * j, 8)
                        gt = kt[:, 2, ts].unsqueeze(2).to_broadcast([P, 8, HE])
                        pool.wait_ge(S("oh1_eq"), b0(1))
                        pool.tensor_tensor(oh1[:, j], oh1[:, j], gt, ALU.mult).then_inc(S("oh1_ready"), 1)

            gates_pool(0)
            for ph_, nxt in (("up0", None), ("down1", 1), ("up1", None)):
                with pool.Fori(0, 16, 1) as i:
                    for j in range(4):
                        lo_split(pool, Tile(ph_, j, i, 4).next(), 0)
                if nxt:
                    gates_pool(1)

            for j in range(9):
                lo_split(pool, Tile("lat", j).next(), 0)
            with pool.Fori(0, 8, 1) as i:
                for j in range(4):
                    lo_split(pool, Tile("conv", j, i, 4).next(), 0)
            with pool.Fori(0, 2, 1) as i:
                for j in range(4):
                    lo_split(pool, Tile("agate", j, i, 4).next(), 0)
            for hh in range(2):
                for j in range(4 - hh):
                    lo_split(pool, Tile(f"mla{hh}", j).next(), 0)
            with pool.Fori(0, 4, 1) as i:
                for j in range(4):
                    lo_split(pool, Tile("aout", j, i, 4).next(), 0)
            for j in range(8):
                lo_split(pool, Tile("k1", j).next(), 0)
            for ph_, cnt in (("q1", 4), ("attn1", 4), ("cout", 3)):
                with pool.Fori(0, cnt, 1) as i:
                    for j in range(4):
                        lo_split(pool, Tile(ph_, j, i, 4).next(), 0)
            for j in range(4):
                lo_split(pool, Tile("cout", 12 + j).next(), 0)

        @block.vector
        def _(dve):
            chain = Sig(dve, S("dve_chain"))
            for b in range(4):
                dve.sem_inc(acc_free[b], 1)
            dve.wait_ge(S("in_ready"), 48)
            chain.link(dve.tensor_scalar(small[:, 0:1], V("qg"), float(P) ** -0.5, None, ALU.mult))
            chain.link(dve.tensor_scalar(small[:, 9:10], V("cqn"), float(P) ** -0.5, None, ALU.mult))
            lo_split(dve, Tile("q", 0), 1)
            W = lambda n: s5w[:, n]
            are, aim = V("ssm_re", 0, 64), V("ssm_im", 0, 64)
            L = chain.link
            dve.wait_ge(S("s5_act"), 1)
            L(dve.tensor_tensor(W(1), are, W(0), ALU.mult))
            L(dve.tensor_tensor(W(2), aim, W(0), ALU.mult))
            L(dve.tensor_scalar(W(3), W(2), float(1 / (2 * np.pi)), None, ALU.mult))
            L(dve.tensor_scalar(W(8), W(3), MAGIC, MAGIC, ALU.add, ALU.subtract))
            L(dve.tensor_tensor(W(4), W(3), W(8), ALU.subtract))
            L(dve.tensor_scalar(W(9), W(4), 0.25, None, ALU.add))
            L(dve.tensor_scalar(W(8), W(9), MAGIC, MAGIC, ALU.add, ALU.subtract))
            L(dve.tensor_scalar(s5_fh, W(4), MAGIC / 4096, MAGIC / 4096, ALU.add, ALU.subtract))
            L(dve.tensor_tensor(s5_fl, W(4), s5_fh, ALU.subtract))
            dve.tensor_tensor(W(5), W(9), W(8), ALU.subtract).then_inc(S("s5_dve"), 1)
            dve.wait_ge(S("s5_act"), 3)
            L(dve.tensor_tensor(W(8), s5_r, W(7), ALU.mult))
            L(dve.tensor_scalar(W(8), W(8), 1.0, None, ALU.subtract))
            L(dve.tensor_tensor(W(9), s5_r, W(6), ALU.mult))
            L(dve.tensor_tensor(W(10), are, are, ALU.mult))
            L(dve.tensor_tensor(W(11), aim, aim, ALU.mult))
            L(dve.tensor_tensor(W(10), W(10), W(11), ALU.add))
            L(dve.reciprocal(W(10), W(10)))
            L(dve.tensor_tensor(W(11), W(8), are, ALU.mult))
            L(dve.tensor_tensor(W(12), W(9), aim, ALU.mult))
            L(dve.tensor_tensor(W(11), W(11), W(12), ALU.add))
            L(dve.tensor_tensor(s5_kr, W(11), W(10), ALU.mult))
            L(dve.tensor_tensor(W(11), W(9), are, ALU.mult))
            L(dve.tensor_tensor(W(12), W(8), aim, ALU.mult))
            L(dve.tensor_tensor(W(11), W(11), W(12), ALU.subtract))
            L(dve.tensor_tensor(s5_ki, W(11), W(10), ALU.mult))

            def norm_apply(r, gain):
                dve.wait_ge(S(f"root{r}"), 1)
                chain.link(dve.reciprocal(rs[:, 1], rs[:, 0]))
                for q in range(4):
                    for k in range(4 * q, 4 * q + 4):
                        m = dve.scalar_tensor_tensor(ht[:, k], X[:, k], V(gain, k), rs[:, 1], ALU.mult, ALU.mult)
                    m.then_inc(S(f"ht_ready{r}"), 1)

            def split_lo(src, dst, hi, done_hi, done, n=4, w=4):
                for q in range(n):
                    dve.wait_ge(done_hi, q + 1)
                    s = slice(w * q, w * q + w)
                    dve.tensor_tensor(dst[:, s], src[:, s], hi[:, s].bitcast(F32), ALU.subtract).then_inc(done, 1)

            norm_apply(0, "mix_g")
            split_lo(ht, h_lo, h_hi, S("h_hi_done0"), S("h_ready0"))
            for j in range(4):
                t = Tile("q", j)
                lo_split(dve, t.next(), 1)
                dve.wait_ge(mm_done, t.done())
                dve.tensor_copy(qku[:, j], bank(t.bank(), T)).then_inc(acc_free[t.bank()], 1)
            with dve.Fori(0, 6, 1) as i:
                for j in range(4):
                    t = Tile("q", j, i, 4, skip=4)
                    lo_split(dve, t.next(), 1)
                    dve.wait_ge(mm_done, t.done())
                    dve.tensor_scalar(qku[:, i * 4 + (j + 4)], bank(t.bank(), T), 1.0, None, ALU.mult).then_inc(acc_free[t.bank()], 1)
            for j in range(4):
                t = Tile("v", j)
                lo_split(dve, t.next(), 1)
                dve.wait_ge(mm_done, t.done())
                dve.tensor_copy(v_tok[:, :, j * P:(j + 1) * P], bank(t.bank(), T).rearrange("p (a n) -> p a n", a=2))\
                    .then_inc(acc_free[t.bank()], 1)
            dve.wait_ge(acc_free[Tile("v", 3).bank()], Tile("v", 3).bank_free() + 1)
            dve.sem_inc(S("qkuv_done"), 1)
            dve.sem_inc(S("scores_done"), 1)
            dve.sem_inc(S("pv_done"), 1)
            with Loop(dve, 4, {chain: 22}) as i:
                dve.wait_ge(S("root5"), i + 1)
                chain.link(dve.reciprocal(rq5[:, 1:5], rq5[:, 1:5]))
                dve.wait_ge(S("act_chain"), i * 2 + 2)
                chain.link(dve.reciprocal(rq5[:, 0], rq5[:, 0]))
                dve.scalar_tensor_tensor(sq5[:, 0], qku[:, i + 16], V("kg"), rq5[:, 0], ALU.mult, ALU.mult)
                dve.scalar_tensor_tensor(sq5[:, 1:5], qku[:, bass.ds(i * 4, 4)], small[:, 0:1], rq5[:, 1:5],
                                         ALU.mult, ALU.mult).then_inc(S("qk_ready"), 1)
                for j in range(4):
                    ta, tb = Tile("gate", 2 * j, i, 8), Tile("gate", 2 * j + 1, i, 8)
                    lo_split(dve, ta.next(), 1)
                    dve.wait_ge(S("scores_done"), i * 4 + (j + 2))
                    chain.link(dve.scalar_tensor_tensor(
                        sco[:].rearrange("p a t -> p (a t)"), C("nd"), Vd("slope", i * 4 + j), bank(4 + j % 2),
                        ALU.mult, ALU.add))
                    chain.link(dve.tensor_reduce(st[:, 0:2], sco[:], AX, ALU.max))
                    dve.tensor_scalar(st[:, 2:4], st[:, 0:2], Vd("sink", i * 4 + j), -1.0, ALU.max, ALU.mult)\
                        .then_inc(e_neg := S("negmax_ready"), 1)
                    lo_split(dve, tb.next(), 1)
                    dve.wait_ge(S("exp_done"), i * 4 + (j + 1))
                    chain.link(dve.tensor_tensor(st[:, 8:10], st[:, 4:6], st[:, 6:8], ALU.add))
                    chain.link(dve.reciprocal(st[:, 10:12], st[:, 8:10]))
                    for b in range(2):
                        m = dve.tensor_scalar(sco[:, b], sco[:, b], st[:, 10 + b:11 + b], None, ALU.mult)
                    m.then_inc(S("prb_ready"), 1)
                    dve.wait_ge(S("pv_done"), i * 4 + (j + 2))
                    chain.link(dve.tensor_scalar(qku[:, i * 4 + j], bank(7, T), 1.0, None, ALU.mult))

            dve.wait_ge(S("dve_chain"), chain.now())
            dve.sem_inc(S("o_ready"), 1)
            split_lo(qku, h_lo, h_hi, S("o_hi_done"), S("o_lo_done"))
            dve.sem_inc(S("y_free"), 1)
            for n in range(2):
                dve.sem_inc(S("rot_used"), 1)
                dve.sem_inc(S("bu_free"), 1)
            dve.wait_ge(S("o_lo_done"), 4)
            TABV = V("tab", 0, 32)

            def cols(a, c0, i):
                a = a[:, 8 * c0:8 * c0 + 8] if i is None else a[:, bass.ds(i * 16 + 8 * c0, 8)]
                return a.unsqueeze(2).to_broadcast([P, 8, 32])

            def phases_dve(c0, i):
                L = chain.link
                tb = TABV.unsqueeze(1).to_broadcast([P, 8, 32])
                fh, fl = cols(s5_fh, c0, i), cols(s5_fl, c0, i)
                L(dve.tensor_tensor(ph[:, 0], fh, tb, ALU.mult))
                L(dve.tensor_scalar(ph[:, 1], ph[:, 0], MAGIC, MAGIC, ALU.add, ALU.subtract))
                L(dve.tensor_tensor(ph[:, 0], ph[:, 0], ph[:, 1], ALU.subtract))
                L(dve.tensor_tensor(ph[:, 1], fl, tb, ALU.mult))
                L(dve.tensor_tensor(ph[:, 0], ph[:, 0], ph[:, 1], ALU.add))
                L(dve.tensor_scalar(ph[:, 1], ph[:, 0], 0.25, None, ALU.add))
                dve.wait_ge(S("tab_ready"), at(c0 + 1, i, 2))
                for f in range(2):
                    L(dve.tensor_scalar(ph[:, 2], ph[:, f], MAGIC, MAGIC, ALU.add, ALU.subtract))
                    m = dve.tensor_tensor(phs[:, f], ph[:, f], ph[:, 2], ALU.subtract)
                    if f == 0:
                        L(m)
                    else:
                        m.then_inc(S("phs_ready"), 1)
                dve.wait_ge(S("phs_ready"), at(c0 + 1, i, 2))

            def coeffs_dve(c0, i):
                L = chain.link
                dve.wait_ge(S("c_loaded"), at(16 * (c0 + 1), i, 32))
                dve.wait_ge(S("out_done"), at(8 * c0 + 1, i, 16))
                kr, ki = cols(s5_kr, c0, i), cols(s5_ki, c0, i)
                co = c_out[:, c0 % 2]
                L(dve.tensor_tensor(ph[:, 0], c_st[:, 0], kr, ALU.mult))
                L(dve.tensor_tensor(ph[:, 1], c_st[:, 1], ki, ALU.mult))
                L(dve.tensor_tensor(co[:, :, 0], ph[:, 0], ph[:, 1], ALU.subtract))
                L(dve.tensor_tensor(co[:, :, 1], ph[:, 1], ph[:, 0], ALU.subtract))
                L(dve.tensor_tensor(ph[:, 0], c_st[:, 0], ki, ALU.mult))
                L(dve.tensor_tensor(ph[:, 1], c_st[:, 1], kr, ALU.mult))
                L(dve.tensor_tensor(ph[:, 0], ph[:, 0], ph[:, 1], ALU.add))
                dve.tensor_scalar(co[:, :, 2], ph[:, 0], -1.0, None, ALU.mult).then_inc(S("c_made"), 1)
                dve.wait_ge(S("c_made"), at(c0 + 1, i, 2))

            def ssm_dve(c0, i):
                c = at(c0, i, 2)
                L = chain.link
                last = i is None and c0 == 7
                for v in range(8):
                    t = Tile("ssm", 8 * c0 + v, i, 16, 4)
                    u = lambda n: at(8 * c0 + v + n, i, 16)
                    rev = v % 2 == 1
                    fl_ = (lambda a: a[:, :, ::-1]) if rev else (lambda a: a)
                    if v in (3, 7):
                        lo_split(dve, Tile("ssm", 8 * c0 + v - 3, i, 16, 4).next(), 1)
                    r = rot[:, v % 2].rearrange("p f a b -> p f (a b)")
                    dve.wait_ge(S("rot_ready"), at(2 * (8 * c0 + v + 1), i, 32))
                    dve.wait_ge(S("bu_done"), u(1))
                    src = fl_(bank(4 + v % 2).rearrange("p (f t) -> p f t", f=2))
                    for f in range(2):
                        m = dve.tensor_tensor(td[:, f], src, r[:, f:f + 1].to_broadcast([P, 2, T]), ALU.mult)
                    m.then_inc(S("bu_free"), 1)
                    dve.wait_ge(S("bu_free"), u(3))
                    dve.tensor_tensor(td[:, 0, 0], td[:, 0, 0], td[:, 1, 1], ALU.add)
                    L(dve.tensor_tensor(td[:, 0, 1], td[:, 0, 1], td[:, 1, 0], ALU.subtract))
                    dec = s5_r[:, bass.ds(c * 8 + v, 1)] if i is not None else s5_r[:, 8 * c0 + v:8 * c0 + v + 1]
                    dec = dec.to_broadcast([P, T])
                    for z in range(2):
                        m = dve.tensor_tensor_scan(td[:, 1, z], dec, td[:, 0, z], 0.0, ALU.mult, ALU.add)
                    L(m)
                    dve.wait_ge(S("out_done"), u(7))
                    for f in range(2):
                        m = dve.tensor_tensor(fl_(pq[:, v % 2, f]), td[:, 1], r[:, f:f + 1].to_broadcast([P, 2, T]),
                                              ALU.mult)
                        if f == 1:
                            m.then_inc(S("rot_used"), 1)
                    dve.wait_ge(S("rot_used"), u(3))
                    dve.sem_inc(S("pq_ready"), 1)
                    if v in (1, 5):
                        t = Tile("ssm", 8 * c0 + v - 1, i, 16, 4)
                        dve.wait_ge(mm_done, t.done())
                        g = gates[:, at(2 * c0 + v // 4, i, 4)]
                        dve.tensor_tensor(g, g, bank(t.bank(), T), ALU.mult).then_inc(acc_free[t.bank()], 1)
                    if v == 3 and not last:
                        phases_dve(c0 + 1, i)
                    if v == 5 and not last:
                        coeffs_dve(c0 + 1, i)
                dve.wait_ge(S("out_done"), at(8 * c0 + 16, i, 16))
                dve.wait_ge(S("gelu_done"), at(c0 + 1, i, 2))
                dcol = V("ssm_d", c0) if i is None else Vd("ssm_d", c)
                dve.scalar_tensor_tensor(us2[:], qku[:, at(20 + c0, i, 2)], dcol, bank(6, T), ALU.mult, ALU.add)\
                    .then_inc(S("y_ready"), 1)
                dve.wait_ge(S("y_ready"), at(c0 + 1, i, 2))
                dve.sem_inc(S("y_free"), 1)

            phases_dve(0, None)
            coeffs_dve(0, None)
            with Loop(dve, 3, {chain: 64}) as i:
                ssm_dve(0, i)
                ssm_dve(1, i)
            ssm_dve(6, None)
            ssm_dve(7, None)
            for q in range(2):
                dve.wait_ge(S("ya_hi_done"), q + 1)
                dve.tensor_tensor(h_lo[:, 4 * q:4 * q + 4], qku[:, 20 + 4 * q:24 + 4 * q],
                                  h_hi[:, 4 * q:4 * q + 4].bitcast(F32), ALU.subtract).then_inc(S("ya_ready"), 1)
            chain.link(dve.tensor_tensor(mods[:, 0], bank(7, 96).rearrange("p (m s) -> p m s", s=2),
                                         V("bmod", 0, 48).unsqueeze(2).to_broadcast([P, 48, 2]), ALU.add))
            dve.sem_inc(S("glu_done"), 2)
            with Loop(dve, 4, {chain: 6}) as i:
                for j in range(2):
                    ta, tb = Tile("glu", 2 * j, i, 4), Tile("glu", 2 * j + 1, i, 4)
                    lo_split(dve, ta.next(), 1)
                    lo_split(dve, tb.next(), 1)
                    dve.wait_ge(S("sg_ready"), i * 2 + (j + 1))
                    chain.link(dve.tensor_tensor(sg[:, j], sg[:, j], bank(ta.bank()), ALU.mult))
                    dve.sem_inc(acc_free[ta.bank()], 1)
                    dve.sem_inc(acc_free[tb.bank()], 1)
                    s2 = sg[:, j].rearrange("p (a t) -> p a t", a=2)
                    chain.link(dve.tensor_tensor(s2, s2, gates[:, bass.ds(i * 4 + (16 + 2 * j), 2)], ALU.mult))
                    g = gates[:, bass.ds(i * 4 + 2 * j, 2)]
                    chain.link(dve.tensor_tensor(g, g, s2, ALU.add))
                    dve.sem_inc(S("glu_done"), 1)
            for q in range(4):
                dve.sem_inc(S("merged_ready"), 1)
            split_lo(gates, h_lo, h_hi, S("m_hi_done"), S("m_ready"))
            with Loop(dve, 4, {}) as i:
                for j in range(4):
                    t = Tile("wout", j, i, 4)
                    lo_split(dve, t.next(), 1)
                    dve.wait_ge(mm_done, t.done())
                    x = X[:, i * 4 + j]
                    dve.tensor_tensor(x, x, bank(t.bank(), T), ALU.add).then_inc(acc_free[t.bank()], 1)
            dve.wait_ge(mm_done, G0["wq"])
            for b in range(4):
                dve.wait_ge(acc_free[b], 1 + A0["wq"] // 4)

            dve.sem_inc(S("x1_ready"), 1)
            norm_apply(1, "ffn_g")
            split_lo(ht, h_lo, h_hi, S("h_hi_done1"), S("h_ready1"))

            def top16(vals, idx, src, tmp):
                L(dve.max(vals[:, 0:8], src))
                dve.max_index(idx[:, 0:8], vals[:, 0:8], src)
                L(dve.match_replace(tmp, vals[:, 0:8], src, LOWEST))
                L(dve.max(vals[:, 8:16], tmp))
                L(dve.max_index(idx[:, 8:16], vals[:, 8:16], tmp))

            for i in range(4):
                for j in range(4):
                    t = Tile("wq", j, i, 4)
                    lo_split(dve, t.next(), 1)
                    dve.wait_ge(S("sub_done"), at(j + 1, i, 4))
                    for tt in range(2):
                        top16(vv[:, j, tt], ii[:, j, tt], bank(4 + j % 2, P, tt * P), mt[:])
                    dve.sem_inc(S("sub_free"), 1)
                w = lambda a: a[:, :, bass.ds(i * 4, 4), :]
                L(dve.tensor_scalar(w(tv), vv[:].rearrange("p j t k -> p t j k"), 1.0, None, ALU.mult))
                L(dve.tensor_scalar(w(ti), ii[:].rearrange("p j t k -> p t j k"), 1.0, None, ALU.mult))
            io16 = C("iota", 0, TOPK).unsqueeze(1).to_broadcast([P, TOPK, TOPK])
            vals, idx = vv[:, 0, 0], ii[:, 0, 0]
            for i in range(PH):
                for tt in range(2):
                    val1, val2, key1, key2 = (a[:, tt, bass.ds(i * 2 + f, 1), :].rearrange("p a k -> p (a k)")
                                      for a in (tv, ti) for f in range(2))
                    rows = lambda a: a.unsqueeze(2).to_broadcast([P, TOPK, TOPK])
                    cols = lambda a: a.unsqueeze(1).to_broadcast([P, TOPK, TOPK])
                    L(dve.tensor_tensor(cand[:], rows(val1), cols(val2), ALU.add))
                    flat = lambda a: a[:].rearrange("p a b -> p (a b)")
                    top16(vals, idx, flat(cand), flat(cand2))
                    L(dve.tensor_scalar(ii[:, 1, 0], idx, 4, None, ALU.logical_shift_right))
                    L(dve.tensor_scalar(ii[:, 2, 0], idx, 15, None, ALU.bitwise_and))
                    for f, kk in ((0, key1), (1, key2)):
                        L(dve.tensor_tensor(eq[:, f], rows(ii[:, 1 + f, 0]), io16, ALU.is_equal))
                        L(dve.tensor_tensor(eq[:, f], eq[:, f], cols(kk), ALU.mult))
                        L(dve.tensor_reduce(vv[:, 1 + f, 0], eq[:, f], AX, ALU.add))
                    L(dve.tensor_scalar(ix[:, tt, 0:2, bass.ds(i * TOPK, TOPK)], vv[:, 1:3, 0], 1.0, None, ALU.mult))
                    L(dve.tensor_scalar(sv[:, tt, i], vals, vals[:, 0:1], None, ALU.subtract))
            dve.sem_inc(S("sel_shifted"), 1)
            dve.wait_ge(S("sel_exp"), 1)
            L(dve.tensor_reduce(mt[:, 0:16], sv[:].rearrange("p a h k -> p (a h) k"), AX, ALU.add))
            L(dve.reciprocal(mt[:, 16:32], mt[:, 0:16]))
            for tt in range(2):
                L(dve.tensor_tensor(ix[:, tt, 2].rearrange("p (h k) -> p h k", k=TOPK), sv[:, tt],
                                    mt[:, 16 + 8 * tt:24 + 8 * tt].unsqueeze(2).to_broadcast([P, PH, TOPK]), ALU.mult))
            dve.sem_inc(S("ix_ready"), 1)
            dve.wait_ge(lo_done[1], N0["down0a"] + 4 * SELECT + 1)
            with dve.Fori(0, 12 - SELECT, 1) as i:
                for j in range(4):
                    lo_split(dve, Tile("down0a", 2 * j, i, 8, 4, skip=8 * SELECT).next(), 1)
            with dve.Fori(0, 4, 1) as i:
                for j in range(4):
                    lo_split(dve, Tile("down0b", j, i, 4).next(), 1)
            for n in range(3):
                dve.wait_ge(S("ix_turned"), n + 1)
                m = dve.tensor_copy(kt[:, n], bank(4 + n, T))
                if n < 2:
                    L(m)
                else:
                    m.then_inc(S("kt_ready"), 1)
            dve.wait_ge(S("kt_ready"), 1)
            L(dve.tensor_tensor(mods[:, 1], bank(7, 96).rearrange("p (m s) -> p m s", s=2),
                                V("bmod", 48, 48).unsqueeze(2).to_broadcast([P, 48, 2]), ALU.add))

            def gates_dve(half):
                dve.wait_ge(S("acts_done"), half + 1)
                dve.wait_ge(acc_free[(A0[f"up{half}"] - 1) % 4], (A0[f"up{half}"] - 1) // 4 + 2)
                cnt = lambda b, i, n: at(2 * 16 * half + b + n, i, 2)
                toks = lambda b, i: slice(8 * b, 8 * b + 8) if i is None else bass.ds(i * 16 + 8 * b, 8)

                def onehots(b, i):
                    dve.wait_ge(S("gate_mm"), cnt(b, i, 1))
                    key1 = kt[:, 0, toks(b, i)].unsqueeze(2).to_broadcast([P, 8, HE])
                    io = C("iota", half * HE, half * HE + HE).unsqueeze(1).to_broadcast([P, 8, HE])
                    dve.tensor_tensor(oh1[:, b % 2], key1, io, ALU.is_equal).then_inc(S("oh1_eq"), 1)
                    key2 = kt[:, 1, toks(b, i)].unsqueeze(2).to_broadcast([P, 8, P])
                    io = C("iota").unsqueeze(1).to_broadcast([P, 8, P])
                    dve.tensor_tensor(oh2[:, b % 2], key2, io, ALU.is_equal).then_inc(S("oh2_ready"), 1)

                def scale(b, i):
                    dve.wait_ge(S("gate_mm"), cnt(b, i, 3))
                    a = ab[:, :, toks(b, i)]
                    dve.tensor_tensor(a, a, bank(4 + b % 2).rearrange("p (t r) -> p r t", r=HE), ALU.mult)\
                        .then_inc(S("gates_in"), 1)

                onehots(0, None)
                with dve.Fori(0, 15, 1) as i:
                    for b in range(2):
                        onehots(b + 1, i)
                        scale(b, i)
                onehots(31, None)
                scale(30, None)
                scale(31, None)
                dve.wait_ge(S("gates_in"), 32 * (half + 1))

            def up_dve(half):
                with Loop(dve, 16, {}) as i:
                    for j in range(4):
                        t = Tile(f"up{half}", j, i, 4)
                        e = lambda n: at(64 * half + j + n, i, 4)
                        dve.wait_ge(S("up_mm"), e(1))
                        dve.tensor_scalar(wp_hi[:, j % 2], ab[:, i * 4 + j], 1.0, None, ALU.mult)\
                            .then_inc(S("wp_hi_done"), 1)
                        dve.wait_ge(S("wp_hi_done"), e(1))
                        dve.tensor_tensor(wp_lo[:, j % 2], ab[:, i * 4 + j], wp_hi[:, j % 2].bitcast(F32),
                                          ALU.subtract).then_inc(S("wp_ready"), 1)
                        lo_split(dve, t.next(), 1)
                dve.wait_ge(mm_done, G0[f"up{half}"] + 64)
                for b in range(8):
                    x = X[:, 2 * b:2 * b + 2]
                    dve.tensor_tensor(x, x, bank(b).rearrange("p (a t) -> p a t", a=2), ALU.add)\
                        .then_inc(S("spilled"), 1)
                dve.wait_ge(S("spilled"), 8 * (half + 1))

            gates_dve(0)
            up_dve(0)
            with dve.Fori(0, 16, 1) as i:
                for j in range(4):
                    lo_split(dve, Tile("down1", j, i, 4).next(), 1)
            gates_dve(1)
            up_dve(1)

            for layer in range(2):
                L(dve.tensor_scalar(mods[:, layer, 16:32], mods[:, layer, 16:32], 1.0, None, ALU.add))
            dve.wait_ge(S("ctx_loaded"), 16)

            def mixer_in(n, xs):
                for q in range(4):
                    for k in range(4 * q, 4 * q + 4):
                        for s_ in range(2):
                            m = dve.tensor_scalar(hm[:, k, s_ * T:(s_ + 1) * T], xs(k, s_), md(n, 1, k, s_),
                                                  md(n, 0, k, s_), ALU.mult, ALU.add)
                    m.then_inc(S("hm_ready"), 1)
                for q in range(4):
                    s_ = slice(4 * q, 4 * q + 4)
                    dve.wait_ge(S("hm_hi"), q + 1 + 4 * n)
                    dve.tensor_tensor(h2_lo[:, s_], hm[:, s_], h2_hi[:, s_].bitcast(F32), ALU.subtract)\
                        .then_inc(S("h2_ready"), 1)

            mixer_in(0, lambda k, s_: (X, xc)[s_][:, k])
            dve.wait_ge(S("x_saved"), 16)
            for j in range(9):
                t = Tile("lat", j)
                lo_split(dve, t.next(), 1)
                dve.wait_ge(mm_done, t.done())
                dve.tensor_copy(lat[:, j] if j < 8 else rk[:], bank(t.bank())).then_inc(acc_free[t.bank()], 1)
                dve.wait_ge(acc_free[t.bank()], t.a0 // 4 + 2)
                dve.sem_inc(S("lat_read"), 1)
            def rotate(x, swapped, tabs, a, n, scratch):
                L(dve.tensor_tensor(scratch, swapped, C(tabs, a, a + n), ALU.mult))
                L(dve.tensor_tensor(x, x, C(tabs, 0, n), ALU.mult))
                L(dve.tensor_tensor(x, x, scratch, ALU.add))

            dve.wait_ge(S("swap_done"), 1)
            rotate(rk[:], bank(5), "rm", N2, N2, cvc[:])
            for f in range(2):
                dve.wait_ge(S("lroot"), f + 1)
                L(dve.reciprocal(lrt[:, f], lrt[:, f]))
                for k in range(4):
                    L(dve.scalar_tensor_tensor(lat[:, 4 * f + k], lat[:, 4 * f + k], V("akvn" if f else "aqn", k),
                                               lrt[:, f], ALU.mult, ALU.mult))
            L(dve.memset(cvu[:], 0.0))
            dve.sem_inc(S("lat_normed"), 1)
            dve.sem_inc(S("cv_done"), 1)
            with Loop(dve, 8, {chain: 6}) as i:
                tb, tc, tu, tg = (Tile("conv", j, i, 4) for j in range(4))
                lo_split(dve, tb.next(), 1)
                lo_split(dve, tc.next(), 1)
                lo_split(dve, tu.next(), 1)
                dve.wait_ge(mm_done, tu.done())
                dve.wait_ge(S("cvc_ready"), at(1, i, 1))
                seq = lambda a: a.rearrange("p (s t) -> p s t", s=2)
                L(dve.tensor_tensor(cvu[:, :, 4:4 + T], seq(cvc[:]), seq(bank(tu.bank())), ALU.mult))
                dve.sem_inc(acc_free[tc.bank()], 1)
                dve.sem_inc(acc_free[tu.bank()], 1)
                a = seq(cva[:])
                w = lambda n: Vd("convw", i + 8 * n)
                L(dve.tensor_scalar(a, cvu[:, :, 3:3 + T], w(0), None, ALU.mult))
                L(dve.scalar_tensor_tensor(a, cvu[:, :, 4:4 + T], w(1), a, ALU.mult, ALU.add))
                L(dve.scalar_tensor_tensor(a, cvu[:, :, 5:5 + T], w(2), a, ALU.mult, ALU.add))
                L(dve.tensor_tensor(cva[:], cva[:], bank(tb.bank()), ALU.mult))
                lo_split(dve, tg.next(), 1)
                dve.sem_inc(acc_free[tb.bank()], 1)
                dve.wait_ge(S("cvg_ready"), at(1, i, 1))
                dve.sem_inc(acc_free[tg.bank()], 1)
                L(dve.tensor_tensor(mx[:, i], cva[:], cvg[:], ALU.mult))
                dve.sem_inc(S("cv_done"), 1)
            with dve.Fori(0, 2, 1) as i:
                for j in range(4):
                    lo_split(dve, Tile("agate", j, i, 4).next(), 1)
            for q in range(4):
                dve.wait_ge(S("lh_done"), q + 1)
                s_ = slice(2 * q, 2 * q + 2)
                dve.tensor_tensor(ll[:, s_], lat[:, s_], lh[:, s_].bitcast(F32), ALU.subtract)\
                    .then_inc(S("ll_done"), 1)
            for hh in range(2):
                for j in range(4 - hh):
                    t = Tile(f"mla{hh}", j)
                    lo_split(dve, t.next(), 1)
                    if j in (1, 2):
                        dve.wait_ge(mm_done, t.done())
                        for m in range(4):
                            dst = kn if j == 1 else vn
                            dve.tensor_copy(dst[:, m], bank((t.a0 + m) % 4)).then_inc(acc_free[(t.a0 + m) % 4], 1)
                if hh == 0:
                    for m in range(4):
                        dve.wait_ge(S("swap_done"), m + 2)
                        rotate(qr[:, m], bank(4 + m % 2), "rm", N2, N2, mrt[:, 0])
                        dve.sem_inc(S("qr_ready"), 1)
                for j in range(4):
                    n = 4 * hh + j
                    b_ = n % 2
                    for b in range(3):
                        dve.wait_ge(S("msc_done"), 3 * n + b + 1)
                        if b < 2:
                            m = dve.tensor_reduce(mst[:, b_, b:b + 1], bank(4 + b), AX, ALU.max, negate=True)
                        else:
                            m = dve.tensor_reduce(mst[:, b_, 2:4], bank(6).rearrange("p (a t) -> p a t", a=2), AX,
                                                  ALU.max, negate=True)
                        m.then_inc(S("mmax_ready"), 1)
                    dve.wait_ge(S("mexp_done"), 3 * n + 3)
                    L(dve.reciprocal(mst[:, b_, 8:12], mst[:, b_, 4:8]))
                    for b in range(2):
                        dve.tensor_scalar(msc[:, b], msc[:, b], mst[:, b_, 8 + b:9 + b], None, ALU.mult)
                    for b in range(2):
                        c_ = msc[:, 2, b * T:(b + 1) * T]
                        m = dve.tensor_scalar(c_, c_, mst[:, b_, 10 + b:11 + b], None, ALU.mult)
                    m.then_inc(S("mprob_ready"), 1)
                    dve.wait_ge(S("mtr_done"), n + 1)
                    dve.tensor_copy(mpt[:, 2], bank(2)).then_inc(S("mpt_dve"), 1)
                    dve.wait_ge(S("mpv_done"), 2 * n + 2)
                    g = mx[:, 8 + n]
                    dve.tensor_tensor(g, g, bank(3), ALU.mult).then_inc(S("mpv_read"), 1)
                    dve.wait_ge(S("mpv_read"), n + 1)
            dve.sem_inc(S("mixed"), 1)

            def dve_out(name, layer, n):
                src = mx if layer == 0 else q1
                for q in range(4):
                    dve.wait_ge(S("mx_hi"), q + 1 + 4 * layer)
                    s_ = slice(4 * q, 4 * q + 4)
                    dve.tensor_tensor(h2_lo[:, s_, 0:n], src[:, s_], h2_hi[:, s_, 0:n].bitcast(F32), ALU.subtract)\
                        .then_inc(S("mx_ready"), 1)
                dve.wait_ge(S("xx_scaled"), 4 + 4 * layer)

                def step(j, i, k):
                    t = Tile(name, j, i, 4)
                    lo_split(dve, t.next(), 1)
                    dve.wait_ge(mm_done, t.done())
                    for s_ in range(n // T):
                        x = XX[:, k, s_ * T:(s_ + 1) * T]
                        gcol = md(layer, 2, k, s_) if i is None else mdd(layer, 2, k, s_)
                        m = dve.scalar_tensor_tensor(x, bank(t.bank(), T, s_ * T), gcol, x, ALU.mult, ALU.add)
                    m.then_inc(acc_free[t.bank()], 1)

                with dve.Fori(0, 4 if layer == 0 else 3, 1) as i:
                    for j in range(4):
                        step(j, i, i * 4 + j)
                if layer:
                    for j in range(4):
                        step(12 + j, None, 12 + j)
                for b in range(4):
                    e = A0[name] + 16 - 4 + b
                    dve.wait_ge(acc_free[e % 4], e // 4 + 2)
                dve.sem_inc(S("z_ready"), 1)
                dve.wait_ge(S("ln_mean"), 1 + layer)
                for q in range(4):
                    x = XX[:, 4 * q:4 * q + 4, 0:n]
                    dve.tensor_tensor(x, x, lnm[:, 0:n].unsqueeze(1).to_broadcast([P, 4, n]), ALU.subtract)\
                        .then_inc(S("ln_cent"), 1)
                dve.wait_ge(S("ln_root"), 1 + layer)
                L(dve.reciprocal(lnr[:, 1, 0:n], lnr[:, 0, 0:n]))
                for q in range(4):
                    for k in range(4 * q, 4 * q + 4):
                        x = XX[:, k, 0:n]
                        m = dve.scalar_tensor_tensor(x, x, V("lng", 16 * layer + k), lnr[:, 1, 0:n], ALU.mult, ALU.mult)
                    L(m)
                    for k in range(4 * q, 4 * q + 4):
                        x = XX[:, k, 0:n]
                        m = dve.tensor_scalar(x, x, V("lnb", 16 * layer + k), None, ALU.add)
                    if layer:
                        m.then_inc(S("out_ready"), 1)
                    else:
                        L(m)

            dve_out("aout", 0, N2)
            mixer_in(1, lambda k, s_: XX[:, k, s_ * T:(s_ + 1) * T])
            dve.wait_ge(S("h2_ready"), 8)

            def head_dve(c1, i, per, n, gain, final):
                r = lambda a: xt(a, 2) if n == N2 else xt(a)
                dve.wait_ge(S("hroot"), at(c1 + 1, i, per))
                L(dve.reciprocal(r(6), r(4)))
                for s_ in range(n // T):
                    m = dve.scalar_tensor_tensor(xt(8 + s_), xt(s_), gain, xt(6 + s_), ALU.mult, ALU.mult)
                m.then_inc(S("hn_ready"), 1)
                dve.wait_ge(S("hswap_done"), at(c1 + 1, i, per))
                L(dve.tensor_tensor(xt(10), bank(5, T), C("rg", T, 2 * T), ALU.mult))
                L(dve.tensor_tensor(xt(11), xt(8), C("rg", 0, T), ALU.mult))
                L(dve.tensor_tensor(final, xt(10), xt(11), ALU.add))

            for j in range(8):
                t = Tile("k1", j)
                lo_split(dve, t.next(), 1)
                dve.wait_ge(mm_done, t.done())
                if j < 4:
                    dve.tensor_copy(k1[:, j], bank(t.bank())).then_inc(acc_free[t.bank()], 1)
                else:
                    dve.tensor_copy(v1[:, :, (j - 4) * P:(j - 3) * P], bank(t.bank()).rearrange("p (a n) -> p a n", a=4))\
                        .then_inc(acc_free[t.bank()], 1)
            for j in range(4):
                dve.wait_ge(acc_free[Tile("k1", 4 + j).bank()], Tile("k1", 4 + j).a0 // 4 + 2)
            for j in range(4):
                L(dve.tensor_copy(xt(0, 2), k1[:, j].rearrange("p (a t) -> p a t", a=2)))
                dve.sem_inc(S("hraw_ready"), 1)
                head_dve(j, None, 0, N2, V("ckn"), k1[:, j, 0:T])
                L(dve.tensor_copy(k1[:, j, T:N2], xt(9)))
            with Loop(dve, 4, {chain: 20}) as i:
                for j in range(4):
                    t = Tile("q1", j, i, 4)
                    dve.wait_ge(mm_done, t.done())
                    L(dve.tensor_copy(xt(0), bank(t.bank(), T)))
                    dve.sem_inc(acc_free[t.bank()], 1)
                    dve.sem_inc(S("hraw_ready"), 1)
                    lo_split(dve, t.next(), 1)
                    head_dve(4 + j, i, 4, T, small[:, 9:10], q1[:, i * 4 + j])
            dve.sem_inc(S("h1_ready"), 1)
            with Loop(dve, 4, {chain: 16}) as i:
                for j in range(4):
                    t = Tile("attn1", j, i, 4)
                    n = lambda k: at(j + k, i, 4)
                    lo_split(dve, t.next(), 1)
                    dve.wait_ge(S("h1pv_done"), n(1))
                    dve.tensor_scalar(xt(4), q1[:, bass.ds(i * 4 + j, 1)], 1.0, None, ALU.mult)\
                        .then_inc(S("qh_ready"), 1)
                    for b in range(2):
                        dve.wait_ge(S("h1sc_done"), at(2 * j + b + 1, i, 8))
                        dve.tensor_reduce(st[:, b:b + 1], bank(4 + b), AX, ALU.max, negate=True)\
                            .then_inc(S("h1max_ready"), 1)
                    dve.wait_ge(S("h1exp_done"), at(2 * j + 2, i, 8))
                    L(dve.reciprocal(st[:, 8:10], st[:, 4:6]))
                    for b in range(2):
                        m = dve.tensor_scalar(xt(6 + 2 * b, 2), xt(6 + 2 * b, 2), st[:, 8 + b:9 + b], None, ALU.mult)
                    m.then_inc(S("h1pr_ready"), 1)
                    dve.wait_ge(S("h1tr_done"), n(1))
                    dve.tensor_copy(xt(12, 2), bank(7).rearrange("p (a t) -> p a t", a=2)).then_inc(S("h1pt_dve"), 1)
                    dve.wait_ge(S("h1pv_done"), n(2))
                    L(dve.tensor_copy(xt(5), bank(6, T)))
                    dve.wait_ge(S("g1_ready"), n(1))
                    dve.sem_inc(acc_free[t.bank()], 1)
                    L(dve.tensor_tensor(xt(5), xt(5), xt(14), ALU.mult))
                    L(dve.tensor_scalar(q1[:, bass.ds(i * 4 + j, 1)], xt(5), 1.0, None, ALU.mult))
            dve.sem_inc(S("mixed"), 1)
            dve_out("cout", 1, T)

        @block.tensor
        def _(pe):
            pe.wait_ge(S("in_ready"), 48)

            def norm_sums(r):
                for q in range(4):
                    pe.wait_ge(S(f"sq_ready{r}"), q + 1)
                    for k in range(4):
                        m = pe.matmul(bank(6, T), C("ones"), sq[:, q % 2, k], start=(q + k == 0), stop=(q + k == 6))
                    m.then_inc(S(f"sum_done{r}"), 1)

            norm_sums(0)
            pe.wait_ge(S("h_ready0"), 4)
            for j in range(4):
                dense(pe, Tile("q", j), xh1, xl1)
            with pe.Fori(0, 6, 1) as i:
                for j in range(4):
                    dense(pe, Tile("q", j, i, 4, skip=4), xh1, xl1)
            for j in range(4):
                t = Tile("v", j)
                wait_weights(pe, t)
                pe.wait_ge(acc_free[t.bank()], t.bank_free())
                for tt in range(2):
                    tok = slice(tt * P, tt * P + P)
                    for k in range(BLK):
                        for n, (x, w) in enumerate(((h_hi, w_hi), (h_hi, w_lo), (h_lo, w_hi))):
                            m = pe.matmul(bank(t.bank(), P, tt * P), x[:, k, tok], w[:, t.par, k],
                                          start=(k + n == 0), stop=(k == BLK - 1 and n == 2))
                m.then_inc(mm_done, 1)
            with pe.Fori(0, 4, 1) as i:
                pe.wait_ge(S("sq5_ready"), i + 1)
                for a in range(2):
                    pe.matmul(bank(4 + a), C("ones"), sq5[:, 1 + 2 * a:3 + 2 * a], start=True, stop=True)
                pe.matmul(bank(6, T), C("ones"), sq5[:, 0], start=True, stop=True).then_inc(S("norm5_done"), 1)
                for j in range(4):
                    ta, tb = Tile("gate", 2 * j, i, 8), Tile("gate", 2 * j + 1, i, 8)
                    dense(pe, ta, xh1, xl1)
                    if j == 0:
                        pe.wait_ge(S("qk_ready"), i + 1)
                        pe.wait_ge(S("vgrp_ready"), i + 1)
                    for b in range(2):
                        m = pe.matmul(bank(4 + j % 2, T, b * T), sq5[:, 1 + j, b * P:(b + 1) * P], sq5[:, 0],
                                      start=True, stop=True)
                    m.then_inc(S("scores_done"), 1)
                    dense(pe, tb, xh1, xl1)
                    pe.wait_ge(S("prb_ready"), i * 4 + (j + 1))
                    for kc in range(2):
                        for b in range(2):
                            m = pe.transpose(bank(6, P, kc * T + b * P), sco[:, b, kc * P:(kc + 1) * P], C("ident"))
                    m.then_inc(S("ptr_done"), 1)
                    pe.wait_ge(S("prt_ready"), i * 4 + (j + 1))
                    for kc in range(2):
                        m = pe.matmul(bank(7, T), v_grp[:, kc], prt[:, kc], start=(kc == 0), stop=(kc == 1))
                    m.then_inc(S("pv_done"), 1)
            pe.wait_ge(S("cs_ready"), 1)
            pe.wait_ge(S("o_lo_done"), 4)
            for n in range(8):
                pe.sem_inc(S("out_done"), 1)

            def bu(c0, v, i):
                u = lambda n: at(8 * c0 + v + n, i, 16)
                if v == 0:
                    pe.wait_ge(S("b_loaded"), at(16 * (c0 + 1), i, 32))
                    pe.wait_ge(S("us_ready"), at(c0 + 1, i, 2))
                pe.wait_ge(S("bu_free"), u(1))
                j, d = v // 2, v % 2
                s_ = slice(32 * j, 32 * j + 32)
                for f in range(2):
                    m = pe.matmul(bank(4 + v % 2, T, f * T), b_st[s_, c0 % 2, d, f], uc[s_, c0 % 2],
                                  start=True, stop=True)
                m.then_inc(S("bu_done"), 1)

            def mod_tile(t, col, i):
                pe.wait_ge(tile_loaded[t.slot], t.loaded())
                for k in range(BLK):
                    o_ = bank(7, 2, 2 * col) if i is None else banks[:, 7, bass.ds(col, 2)]
                    m = pe.matmul(o_, ring[:, t.slot, k], cs[:, k], start=(k == 0), stop=(k == BLK - 1))
                m.then_inc(mm_done, 1)

            def ssm_pe(c0, i):
                for v in range(8):
                    t = Tile("ssm", 8 * c0 + v, i, 16, 4)
                    if v < 7:
                        bu(c0, v + 1, i)
                    elif not (i is None and c0 == 7):
                        bu(c0 + 1, 0, i)
                    if v % 4 == 0:
                        dense(pe, t, xh1, xl1)
                    else:
                        md = 6 * c0 + v - 1 - v // 4
                        mod_tile(t, md if i is None else i * 24 + 2 * md, i)
                    if v:
                        ssm_out(c0, v - 1, i)
                ssm_out(c0, 7, i)

            def ssm_out(c0, v, i):
                j = v // 2
                pe.wait_ge(S("pq_ready"), at(8 * c0 + v + 1, i, 16))
                if v == 0:
                    pe.wait_ge(S("y_free"), at(c0 + 1, i, 2))
                for n, (sel, f, z) in enumerate(((0, 0, 0), (2, 0, 1), (2, 1, 0), (1, 1, 1))):
                    m = pe.matmul(banks[32 * j:32 * j + 32, 6, 0:T], c_out[:, c0 % 2, v, sel], pq[:, v % 2, f, z],
                                  start=(v % 2 == 0 and n == 0), stop=(v % 2 == 1 and n == 3))
                m.then_inc(S("out_done"), 1)

            bu(0, 0, None)
            with pe.Fori(0, 3, 1) as i:
                ssm_pe(0, i)
                ssm_pe(1, i)
            ssm_pe(6, None)
            ssm_pe(7, None)
            pe.wait_ge(S("ya_ready"), 2)
            with pe.Fori(0, 4, 1) as i:
                for j in range(4):
                    t = Tile("glu", j, i, 4)
                    wait_weights(pe, t)
                    pe.wait_ge(acc_free[t.bank()], t.bank_free())
                    for half in range(2):
                        for k in range(8):
                            for n, (w, x) in enumerate(((w_hi, h_hi), (w_lo, h_hi), (w_hi, h_lo))):
                                m = pe.matmul(bank(t.bank(), T, half * T), w[:, t.par, 2 * k + half], x[:, k],
                                              start=(k + n == 0), stop=(k == 7 and n == 2))
                    m.then_inc(mm_done, 1)
            pe.wait_ge(S("m_ready"), 4)
            with pe.Fori(0, 4, 1) as i:
                for j in range(4):
                    dense(pe, Tile("wout", j, i, 4), xh1, xl1)
            norm_sums(1)
            pe.wait_ge(S("h_ready1"), 4)
            pe.wait_ge(S("sk_loaded"), 16)
            pe.sem_inc(S("qs_used"), 4)
            def sub_scores(j, i):
                pe.wait_ge(acc_free[Tile("wq", j).bank()], at(A0["wq"] // 4 + (A0["wq"] % 4 + j) // 4 + 2, i, 1))
                pe.wait_ge(S("sub_free"), at(j + 1, i, 4))
                for tt in range(2):
                    m = pe.matmul(bank(4 + j % 2, P, tt * P), qs[:, j, tt * P:(tt + 1) * P], sk[:, i * 4 + j],
                                  start=True, stop=True)
                m.then_inc(S("sub_done"), 1)
                pe.wait_ge(S("sub_done"), at(j + 1, i, 4))
                pe.sem_inc(S("qs_used"), 1)

            pe.sem_inc(S("sub_free"), 2)
            with pe.Fori(0, 4, 1) as i:
                for j in range(4):
                    dense(pe, Tile("wq", j, i, 4), xh1, xl1)
                    if j:
                        sub_scores(j - 1, i)
                sub_scores(3, i)
            with pe.Fori(0, 12, 1) as i:
                for j in range(4):
                    dense(pe, Tile("down0a", 2 * j, i, 8, 4), xh1, xl1)
                    mod_tile(Tile("down0a", 2 * j + 1, i, 8, 4), i * 8 + 2 * j, i)
            with pe.Fori(0, 4, 1) as i:
                for j in range(4):
                    dense(pe, Tile("down0b", j, i, 4), xh1, xl1)
            pe.wait_ge(S("ix_ready"), 1)
            for n in range(3):
                for tt in range(2):
                    m = pe.transpose(bank(4 + n, P, tt * P), ix[:, tt, n], C("ident"))
                m.then_inc(S("ix_turned"), 1)
            pe.wait_ge(S("kt_ready"), 1)
            pe.sem_inc(S("gate_mm"), 2)
            pe.sem_inc(S("up_mm"), 2)

            def gates_pe(half):
                with pe.Fori(0, 16, 1) as i:
                    for j in range(2):
                        b0 = lambda n: at(2 * 16 * half + j + n, i, 2)
                        pe.wait_ge(S("oh1_ready"), b0(1))
                        pe.wait_ge(S("oh2_ready"), b0(1))
                        for t in range(8):
                            m = pe.matmul(bank(4 + j, HE, t * HE), oh2[:, j, t], oh1[:, j, t], start=True, stop=True)
                        m.then_inc(S("gate_mm"), 1)

            def up_pe(half):
                pe.wait_ge(S("gates_in"), 32 * (half + 1))
                for b in range(4):
                    a = A0[f"up{half}"] + b
                    pe.wait_ge(acc_free[a % 4], a // 4 + 1)

                def tile(j, i, first):
                    t = Tile(f"up{half}", j, i, 4, skip=0 if first else 4)
                    wait_weights(pe, t)
                    pe.wait_ge(S("wp_ready"), at(64 * half + j + 1 + (0 if first else 4), i, 4))
                    for k in range(BLK):
                        for n, (w, x) in enumerate(((w_hi, wp_hi), (w_lo, wp_hi), (w_hi, wp_lo))):
                            m = pe.matmul(bank(k // 2, T, k % 2 * T), w[:, t.par, k], x[:, j % 2],
                                          start=(first and j == 0 and n == 0 and k % 2 == 0), stop=False,
                                          skip_group_check=True)
                    m.then_inc(mm_done, 1)
                    pe.wait_ge(mm_done, t.done())
                    pe.sem_inc(S("up_mm"), 1)

                for j in range(4):
                    tile(j, None, True)
                with pe.Fori(0, 15, 1) as i:
                    for j in range(4):
                        tile(j, i, False)

            gates_pe(0)
            up_pe(0)
            pe.wait_ge(S("spilled"), 8)
            with pe.Fori(0, 16, 1) as i:
                for j in range(4):
                    dense(pe, Tile("down1", j, i, 4), xh1, xl1)
            gates_pe(1)
            up_pe(1)
            pe.wait_ge(S("spilled"), 16)
            def xh2(k): return h2_hi[:, k]
            def xl2(k): return h2_lo[:, k]
            pe.wait_ge(S("h2_ready"), 4)
            for j in range(9):
                dense(pe, Tile("lat", j), xh2, xl2, N2)
            pe.wait_ge(S("lat_read"), 9)
            pe.matmul(bank(5), C("perm_m"), rk[:], start=True, stop=True).then_inc(S("swap_done"), 1)
            for k in range(8):
                pe.wait_ge(S("lsq_ready"), k + 1)
                pe.matmul(bank(6 + k // 4), C("ones"), lsq[:, k % 2], start=(k % 4 == 0), stop=(k % 4 == 3))\
                    .then_inc(S("lsum_done"), 1)
            with pe.Fori(0, 8, 1) as i:
                for j in range(4):
                    dense(pe, Tile("conv", j, i, 4), xh2, xl2, N2)
            with pe.Fori(0, 2, 1) as i:
                for j in range(4):
                    dense(pe, Tile("agate", j, i, 4), xh2, xl2, N2)
            pe.wait_ge(S("ll_done"), 4)
            for hh in range(2):
                if hh:
                    pe.wait_ge(S("mpv_read"), 4)
                for j in range(4 - hh):
                    t = Tile(f"mla{hh}", j)
                    wait_weights(pe, t)
                    c0 = 0 if j in (0, 3) else 4
                    for m in range(4):
                        a = t.a0 + m
                        pe.wait_ge(acc_free[a % 4], a // 4 + 1)
                        for kc in range(4):
                            for n, (w, x) in enumerate(((w_hi, lh), (w_lo, lh), (w_hi, ll))):
                                f = dict(start=(kc + n == 0), stop=(kc == 3 and n == 2))
                                if j == 2:
                                    mm = pe.matmul(bank(a % 4), x_tok(lh if n < 2 else ll, c0 + kc, m),
                                                   w[:, t.par, 4 * kc:4 * kc + 4], **f)
                                else:
                                    mm = pe.matmul(bank(a % 4), w[:, t.par, 4 * kc + m], x[:, c0 + kc], **f)
                    mm.then_inc(mm_done, 1)
                last = Tile(f"mla{hh}", 3 - hh)
                for m in range(4):
                    a = last.a0 + m
                    pe.wait_ge(acc_free[a % 4], a // 4 + 2)
                if hh == 0:
                    for m in range(4):
                        if m >= 2:
                            pe.wait_ge(S("qr_ready"), m - 1)
                        pe.matmul(bank(4 + m % 2), C("perm_m"), qr[:, m], start=True, stop=True)\
                            .then_inc(S("swap_done"), 1)
                    pe.wait_ge(S("qr_ready"), 4)
                for j in range(4):
                    n = 4 * hh + j
                    hp = slice(64 * (n % 2), 64 * (n % 2) + 64)
                    for b in range(4):
                        if n and b < 3:
                            pe.wait_ge(S("mexp_done"), 3 * (n - 1) + b + 1)
                        qt = slice(b * P, (b + 1) * P)
                        o_, ks = (bank(4 + b), slice(0, N2)) if b < 2 else (bank(6, T, (b - 2) * T), slice(T, N2))
                        pe.matmul(o_, qn[:, j, qt], kn[:, j, ks], start=True, stop=False)
                        mm = pe.matmul(o_, qr[hp, n // 2, qt], rk[hp, ks], start=False, stop=True)
                        if b != 2:
                            mm.then_inc(S("msc_done"), 1)
                    pe.wait_ge(S("mprob_ready"), n + 1)
                    for kc in range(4):
                        for b in range(2):
                            pe.transpose(bank(kc // 2, P, kc % 2 * T + b * P), msc[:, b, kc * P:(kc + 1) * P], C("ident"))
                    for kc in range(2):
                        for b in range(2):
                            mm = pe.transpose(bank(2, P, kc * T + b * P),
                                              msc[:, 2, b * T + kc * P:b * T + (kc + 1) * P], C("ident"))
                    mm.then_inc(S("mtr_done"), 1)
                    if n:
                        pe.wait_ge(S("mpv_read"), n)
                    for kc in range(4):
                        if kc % 2 == 0:
                            pe.wait_ge(S("mpt_act"), 2 * n + kc // 2 + 1)
                        mm = pe.matmul(bank(3, T), vn[:, kc, j * P:(j + 1) * P], mpt[:, kc // 2, kc % 2 * T:(kc % 2 + 1) * T],
                                       start=(kc == 0), stop=(kc == 3))
                    mm.then_inc(S("mpv_done"), 1)
                    pe.wait_ge(S("mpt_dve"), n + 1)
                    for kc in range(2):
                        mm = pe.matmul(bank(3, T, T), vn[:, 2 + kc, j * P:(j + 1) * P], mpt[:, 2, kc * T:(kc + 1) * T],
                                       start=(kc == 0), stop=(kc == 1))
                    mm.then_inc(S("mpv_done"), 1)

            def pe_out(name, layer, n):
                pe.wait_ge(S("mx_ready"), 4 + 4 * layer)
                xh, xl = (lambda k: h2_hi[:, k, 0:n]), (lambda k: h2_lo[:, k, 0:n])
                with pe.Fori(0, 4 if layer == 0 else 3, 1) as i:
                    for j in range(4):
                        dense(pe, Tile(name, j, i, 4), xh, xl, n)
                if layer:
                    for j in range(4):
                        dense(pe, Tile(name, 12 + j), xh, xl, n)
                pe.wait_ge(S("z_ready"), 1 + layer)
                for k in range(16):
                    mm = pe.matmul(bank(6, n), C("ones"), XX[:, k, 0:n], start=(k == 0), stop=(k == 15))
                mm.then_inc(S("ln_sum"), 1)
                for q in range(4):
                    pe.wait_ge(S("ln_sq"), q + 1 + 4 * layer)
                    for k in range(4):
                        mm = pe.matmul(bank(7, n), C("ones"), lns[:, q % 2, k, 0:n], start=(q + k == 0), stop=(q + k == 6))
                    mm.then_inc(S("ln_sqsum"), 1)

            pe_out("aout", 0, N2)
            pe.wait_ge(S("h2_ready"), 8)
            for j in range(4):
                dense(pe, Tile("k1", j), xh2, xl2, N2)
            for j in range(4):
                t = Tile("v1", j)
                wait_weights(pe, t)
                pe.wait_ge(acc_free[t.bank()], t.bank_free())
                for tt in range(4):
                    for k in range(BLK):
                        for n, (x, w) in enumerate(((h2_hi, w_hi), (h2_hi, w_lo), (h2_lo, w_hi))):
                            m = pe.matmul(bank(t.bank(), P, tt * P), x_tok(x, k, tt), w[:, t.par, k],
                                          start=(k + n == 0), stop=(k == BLK - 1 and n == 2))
                m.then_inc(mm_done, 1)

            def head_pe(c1, i, per, n):
                pe.wait_ge(S("hsq_ready"), at(c1 + 1, i, per))
                sq_ = xt(2, 2) if n == N2 else xt(2)
                pe.matmul(bank(4, n), C("ones"), sq_, start=True, stop=True).then_inc(S("hsum_done"), 1)
                pe.wait_ge(S("hn_ready"), at(c1 + 1, i, per))
                pe.matmul(bank(5, T), C("perm_g"), xt(8), start=True, stop=True).then_inc(S("hswap_done"), 1)

            for j in range(4):
                head_pe(j, None, 0, N2)
            xh, xl = (lambda k: h2_hi[:, k, 0:T]), (lambda k: h2_lo[:, k, 0:T])
            with pe.Fori(0, 4, 1) as i:
                for j in range(4):
                    dense(pe, Tile("q1", j, i, 4), xh, xl)
                    head_pe(4 + j, i, 4, T)
            pe.wait_ge(S("h1_ready"), 1)
            pe.sem_inc(S("h1pv_done"), 1)
            with pe.Fori(0, 4, 1) as i:
                for j in range(4):
                    t = Tile("attn1", j, i, 4)
                    c_ = lambda k: at(j + k, i, 4)
                    if j == 0:
                        pe.wait_ge(S("kg_ready"), at(1, i, 1))
                        pe.wait_ge(S("vg_ready"), at(1, i, 1))
                    pe.wait_ge(S("qh_ready"), c_(1))
                    for b in range(2):
                        pe.matmul(bank(4 + b), XX[:, 4, T + b * P:T + (b + 1) * P], xt(0, 2), start=True, stop=True)\
                            .then_inc(S("h1sc_done"), 1)
                    dense(pe, t, xh, xl)
                    pe.wait_ge(S("h1pr_ready"), c_(1))
                    for kc in range(4):
                        for b in range(2):
                            m = pe.transpose(bank(6 + kc // 2, P, kc % 2 * T + b * P),
                                             XX[:, 6 + 2 * b + kc // 2, T + kc % 2 * P:T + (kc % 2 + 1) * P], C("ident"))
                    m.then_inc(S("h1tr_done"), 1)
                    pe.wait_ge(S("h1pt_act"), c_(1))
                    pe.wait_ge(S("h1pt_dve"), c_(1))
                    for kc in range(4):
                        m = pe.matmul(bank(6, T), XX[:, 2 + kc // 2, T + kc % 2 * P:T + (kc % 2 + 1) * P], xt(10 + kc),
                                      start=(kc == 0), stop=(kc == 3))
                    m.then_inc(S("h1pv_done"), 1)
            pe_out("cout", 1, T)


def lay_out(inp):
    f = np.float32
    A = {k: np.asarray(v) for k, v in inp.items()}

    def tiles(w):
        k, n = w.shape
        return w.reshape(k // P, P, n // P, P).transpose(2, 1, 0, 3).reshape(n // P, P, BLK * P)

    def tiles_k(w, per):
        k, n = w.shape
        return w.reshape(k // P, P, n // (per * P), per * P).transpose(2, 1, 0, 3).reshape(-1, P, BLK * P)

    w = tiles(A["w_in"][0])
    parts = [w[0:16], w[16:20], w[24:32], w[20:24], w[32:64]]
    wo, md0 = tiles(A["w_attn_o"][0]), tiles(A["w_mod_2"][0])
    for m in range(16):
        parts += [wo[m:m + 1], md0[3 * m:3 * m + 3]]
    ga, gb = tiles_k(A["glu_w_a"][0], 2), tiles_k(A["glu_w_b"][0], 2)
    parts += [np.stack([ga, gb], 1).reshape(16, P, BLK * P)]
    parts += [tiles(A["w_out"][0]), tiles(A["peer_w_query"][0])]
    down = A["peer_down"][0].reshape(P, P, KC, P).transpose(0, 3, 2, 1).reshape(P, P, BLK * P)
    up = A["peer_up"][0].reshape(P, P, D)
    md1 = tiles(A["w_mod_2"][1])
    parts += [np.stack([down[:48], md1], 1).reshape(96, P, BLK * P)]
    parts += [down[48:64], up[0:64], down[64:], up[64:]]
    a = A["a_w_in_2"][0]
    rope = a[:, 4096:4160]
    parts += [tiles(np.concatenate([a[:, 3072:4096], rope, rope], 1))]
    cb, cc, cu, cg = (tiles(a[:, s:s + 1024]) for s in (0, 1024, 2048, 4160))
    parts += [np.stack([cb, cc, cu, cg], 1).reshape(32, P, BLK * P), tiles(a[:, 5184:])]
    qb = A["a_w_qb_2"][0].reshape(512, MLAH, 192)
    kvb = A["a_w_kvb_2"][0].reshape(512, MLAH, 256)
    for hh in range(2):
        s = slice(4 * hh, 4 * hh + 4)
        parts += [tiles_k(qb[:, s, :128].reshape(512, 512), 4), tiles_k(kvb[:, s, :128].reshape(512, 512), 4),
                  tiles_k(kvb[:, s, 128:].reshape(512, 512), 4)]
        if hh == 0:
            parts += [tiles_k(qb[:, :, 128:].reshape(512, 512), 4)]
    parts += [tiles(A["a_w_out_2"][0])]
    c = tiles(A["c_w_in_2"][0])
    parts += [c[16:20], c[20:24], c[0:16], c[24:40], tiles(A["c_w_out_2"][0])]
    stream = np.concatenate(parts)
    assert stream.shape[0] == NTILES, (stream.shape, NTILES)

    def feat(v):
        return np.asarray(v).reshape(-1, P).T

    V = np.zeros((P, NVEC), f)

    def put(name, a):
        s, n = VEC[name]
        V[:, s:s + n] = a

    put("mix_g", feat(A["mix_norm_g"][0])); put("qg", feat(A["q_norm_g"][0])); put("kg", feat(A["k_norm_g"][0]))
    put("sink", np.broadcast_to(A["attn_sink"][0], (P, 16))); put("ffn_g", feat(A["ffn_norm_g"][0]))
    for nm, key in (("ssm_re", "ssm_a_re"), ("ssm_im", "ssm_a_im")):
        put(nm, A[key][0].reshape(2, 8, 4, 2, 64).transpose(3, 4, 1, 2, 0).reshape(P, 64))
    ls = np.broadcast_to(A["ssm_log_step"][0].reshape(2, 8, 4, 2, 1), (2, 8, 4, 2, 64))
    put("ssm_ls", ls.transpose(3, 4, 1, 2, 0).reshape(P, 64))
    put("ssm_d", feat(A["ssm_d"][0]))
    put("cvec", np.stack([feat(A["c_2"][0]), feat(A["c_ctx_2"])], 2).reshape(P, 32))
    put("bmod", np.concatenate([feat(A["b_mod_2"][0]), feat(A["b_mod_2"][1])], 1))
    put("lng", np.concatenate([feat(A["ln_g_2"][0]), feat(A["ln_g_2"][1])], 1))
    put("lnb", np.concatenate([feat(A["ln_b_2"][0]), feat(A["ln_b_2"][1])], 1))
    put("convw", np.concatenate([feat(A["a_conv_w_2"][0][n]) for n in range(3)], 1))
    put("aqn", feat(A["a_q_norm_2"][0])); put("akvn", feat(A["a_kv_norm_2"][0]))
    put("cqn", feat(A["c_q_norm_2"][0])); put("ckn", feat(A["c_k_norm_2"][0]))
    put("slope", np.exp2(-8.0 * (np.arange(16) + 1.0) / 16).astype(f)[None])
    put("eps", f(EPS)); put("halfpi", f(np.pi / 2))
    put("tab", np.concatenate([np.arange(16) * 16, np.arange(16)]).astype(f)[None])
    Cc = np.zeros((P, NCONST), f)

    def putc(name, a):
        s, n = CONST[name]
        Cc[:, s:s + n] = a

    r = np.arange(P)
    putc("ident", np.eye(P, dtype=f)); putc("ones", 1.0); putc("iota", r[None].astype(f))
    q = r[:, None, None] + P * np.arange(2)[None, :, None]
    dist = np.abs(q - np.arange(T)[None, None])
    putc("nd", np.where(dist <= P, -dist.astype(f), f(NEG)).reshape(P, 2 * T))
    t = np.arange(T)
    pos = np.stack([t // 64, t % 64]).astype(f)

    def rope_tab(half):
        inv = (f(10000.0) ** (-np.arange(half, dtype=f) / f(half))).astype(f)
        cos, sin = [], []
        for ax in range(2):
            ang = (pos[ax][:, None] * inv[None]).astype(f).T
            cos += [np.cos(ang), np.cos(ang)]
            sin += [-np.sin(ang), np.sin(ang)]
        return np.concatenate(cos), np.concatenate(sin)

    cm, sm = rope_tab(16)
    one, zero = np.ones((64, T), f), np.zeros((64, T), f)
    cm, sm = np.concatenate([cm, one], 1), np.concatenate([sm, zero], 1)
    putc("rm", np.concatenate([np.tile(cm, (2, 1)), np.tile(sm, (2, 1))], 1))
    putc("rg", np.concatenate(rope_tab(32), 1))

    def perm(half):
        m = np.zeros((P, P), f)
        for b in range(0, P, 2 * half):
            for j in range(half):
                m[b + j + half, b + j] = m[b + j, b + j + half] = 1.0
        return m

    putc("perm_m", perm(16)); putc("perm_g", perm(32))
    x = A["x"][0].reshape(T, KC, P).transpose(2, 1, 0)
    ctx = A["ctx_2"][0].reshape(T, KC, P).transpose(2, 1, 0)
    B = np.zeros((8, 4, 2, 16, 2, 2, 2, 64), f)
    Cm = np.zeros((8, 4, 2, 2, 64, 2, 2, 16), f)
    for ri, (bk, ck) in enumerate((("ssm_b_re", "ssm_c_re"), ("ssm_b_im", "ssm_c_im"))):
        b = A[bk][0].reshape(2, 8, 4, 2, 64, 16)
        cc_ = A[ck][0].reshape(2, 8, 4, 2, 16, 64)
        for g in range(2):
            B[:, :, g, :, :, ri, g, :] = b[:, :, :, g].transpose(1, 2, 4, 0, 3)
            Cm[:, :, :, g, :, ri, g, :] = cc_[:, :, :, g].transpose(1, 2, 0, 4, 3)
    ssm_b = B.reshape(8, P, 2, 2, P)
    ssm_c = Cm.reshape(8, 8, P, 2, 32).transpose(0, 2, 3, 1, 4)
    sk = np.stack([A["peer_sub_keys_1"][0], A["peer_sub_keys_2"][0]], 1)
    sk = sk.reshape(16, P, P).transpose(2, 0, 1)
    c_ = np.ascontiguousarray
    return {"stream": c_(stream.reshape(NTILES, P, BLK, P)), "vecs": V, "consts": Cc, "x_in": c_(x),
            "ctx_in": c_(ctx), "ssm_b": c_(ssm_b), "ssm_c": c_(ssm_c), "subkeys": c_(sk)}


def kernel(**inputs):
    import concourse.bacc as bacc
    from concourse.bass_utils import run_bass_kernel_spmd

    nc = bacc.Bacc("TRN2", target_bir_lowering=False, num_devices=1)
    arrays, args = {}, {}
    for name, a in lay_out(inputs).items():
        arrays[f"in_{name}_dram"] = a
        args[name] = nc.dram_tensor(f"in_{name}_dram", a.shape, F32, kind="ExternalInput").ap()
    out = nc.dram_tensor("out_0_dram", [P, KC, T], F32, kind="ExternalOutput").ap()
    build(nc, **args, out=out)
    got = run_bass_kernel_spmd(nc, [arrays], core_ids=[0]).results[0]["out_0_dram"]
    return np.ascontiguousarray(got.transpose(2, 1, 0)).reshape(1, T, D)
```
